# Optimizing a Trainium2 kernel written in Bass

```python
import jax, jax.numpy as jnp
from jax import lax
import numpy as np

D_MODEL = 1024
BATCH = 1
SEQ = 256
DEPTH = 1

CHUNK = 64
N_META = 16
META_PAD = CHUNK - N_META
ATTN_HEADS = 8
ATTN_KV_HEADS = 2
ATTN_GROUP = ATTN_HEADS // ATTN_KV_HEADS
ATTN_HEAD_DIM = 64
ATTN_WIDTH = ATTN_HEADS * ATTN_HEAD_DIM
KV_WIDTH = ATTN_KV_HEADS * ATTN_HEAD_DIM
WINDOW = 128
WINDOW_CHUNKS = WINDOW // CHUNK
N_PREV = WINDOW_CHUNKS - 1
RET_HEADS = 4
RET_HEAD_DIM = 128
RET_WIDTH = RET_HEADS * RET_HEAD_DIM
MIX_WIDTH = ATTN_WIDTH + RET_WIDTH
IN_WIDTH = ATTN_WIDTH + 2 * KV_WIDTH + 4 * RET_WIDTH
N_EXPERTS = 32
TOP_K = 4
D_FF = D_MODEL
SWIGLU_LIMIT = 7.0
SWIGLU_ALPHA = 1.702
NORM_EPS = 1e-5
NEG_INF = -1e30

kernel_name = "hybrid_swa_retention_moe_block"

def _rms_norm(x, g):
    xf = x.astype(jnp.float32)
    return xf * lax.rsqrt(jnp.mean(xf * xf, axis=-1, keepdims=True) + NORM_EPS) * g.astype(jnp.float32)

def _alibi_slopes(n_heads):
    return jnp.asarray(2.0 ** (-8.0 * np.arange(1, n_heads + 1) / n_heads), dtype=jnp.float32)

def _band_chunks(t, n_prev):
    nc = t.shape[1]
    parts = []
    for j in range(n_prev, 0, -1):
        parts.append(jnp.concatenate([jnp.zeros_like(t[:, :j]), t[:, :nc - j]], axis=1))
    parts.append(t)
    return jnp.concatenate(parts, axis=2)

def _swa_sink_attention(q, k, v, q_gain, k_gain, sinks):
    B, L = q.shape[:2]
    nc = L // CHUNK
    q = _rms_norm(q, q_gain)
    k = _rms_norm(k, k_gain)
    v = v.astype(jnp.float32)
    qc = q.reshape(B, nc, CHUNK, ATTN_KV_HEADS, ATTN_GROUP, ATTN_HEAD_DIM)
    kc = k.reshape(B, nc, CHUNK, ATTN_KV_HEADS, ATTN_HEAD_DIM)
    vc = v.reshape(B, nc, CHUNK, ATTN_KV_HEADS, ATTN_HEAD_DIM)
    meta_shape = (B, nc, N_META, ATTN_KV_HEADS, ATTN_HEAD_DIM)
    keys = jnp.concatenate([jnp.broadcast_to(k[:, None, META_PAD:CHUNK], meta_shape), _band_chunks(kc, N_PREV)], axis=2)
    vals = jnp.concatenate([jnp.broadcast_to(v[:, None, META_PAD:CHUNK], meta_shape), _band_chunks(vc, N_PREV)], axis=2)
    chunk_idx = jnp.arange(nc, dtype=jnp.int32)
    q_pos = jnp.arange(L, dtype=jnp.int32).reshape(nc, CHUNK)
    band_pos = chunk_idx[:, None] * CHUNK + jnp.arange(-N_PREV * CHUNK, CHUNK, dtype=jnp.int32)[None, :]
    meta_pos = jnp.broadcast_to(META_PAD + jnp.arange(N_META, dtype=jnp.int32)[None, :], (nc, N_META))
    key_pos = jnp.concatenate([meta_pos, band_pos], axis=1)
    meta_valid = jnp.broadcast_to((chunk_idx > N_PREV)[:, None], (nc, N_META))
    key_valid = jnp.concatenate([meta_valid, band_pos >= META_PAD], axis=1)
    scores = jnp.einsum('bnqgrd,bnkgd->bgrnqk', qc, keys) * (ATTN_HEAD_DIM ** -0.5)
    dist = jnp.abs(q_pos[:, :, None] - key_pos[:, None, :]).astype(jnp.float32)
    slopes = _alibi_slopes(ATTN_HEADS).reshape(ATTN_KV_HEADS, ATTN_GROUP)
    scores = scores - slopes[:, :, None, None, None] * dist
    scores = jnp.where(key_valid[:, None, :], scores, NEG_INF)
    sink_col = jnp.broadcast_to(sinks.astype(jnp.float32).reshape(ATTN_KV_HEADS, ATTN_GROUP, 1, 1, 1),
                                scores.shape[:-1] + (1,))
    probs = jax.nn.softmax(jnp.concatenate([scores, sink_col], axis=-1), axis=-1)[..., :-1]
    out = jnp.einsum('bgrnqk,bnkgd->bnqgrd', probs, vals)
    return out.reshape(B, L, ATTN_WIDTH)

def _retention(q, k, v):
    B, L = q.shape[:2]
    nc = L // CHUNK
    log_g = jnp.log1p(-(2.0 ** (-5.0 - jnp.arange(RET_HEADS, dtype=jnp.float32))))
    idx = jnp.arange(CHUNK, dtype=jnp.float32)
    diff = idx[:, None] - idx[None, :]
    decay_intra = jnp.where(diff >= 0, jnp.exp(log_g[:, None, None] * jnp.maximum(diff, 0.0)), 0.0)
    zeta = jnp.exp(log_g[:, None] * (CHUNK - 1 - idx)[None, :])
    xi = jnp.exp(log_g[:, None] * (idx + 1)[None, :])
    chunk_decay = jnp.exp(log_g * CHUNK)
    qc = q.reshape(B, nc, CHUNK, RET_HEADS, RET_HEAD_DIM)
    kc = k.reshape(B, nc, CHUNK, RET_HEADS, RET_HEAD_DIM)
    vc = v.reshape(B, nc, CHUNK, RET_HEADS, RET_HEAD_DIM)
    att = jnp.einsum('bnihd,bnjhd->bnhij', qc, kc) * decay_intra
    intra = jnp.einsum('bnhij,bnjhe->bnihe', att, vc)
    kv = jnp.einsum('bnjhd,bnjhe,hj->nbhde', kc, vc, zeta)

    def step(state, kv_n):
        return chunk_decay[None, :, None, None] * state + kv_n, state

    init = jnp.zeros((B, RET_HEADS, RET_HEAD_DIM, RET_HEAD_DIM), jnp.float32)
    _, prev_states = lax.scan(step, init, kv)
    cross = jnp.einsum('bnihd,nbhde->bnihe', qc, prev_states) * xi.T[:, :, None]
    return (intra + cross).reshape(B, L, RET_HEADS, RET_HEAD_DIM)

def _group_norm_heads(x, g):
    mu = jnp.mean(x, axis=-1, keepdims=True)
    xc = x - mu
    var = jnp.mean(xc * xc, axis=-1, keepdims=True)
    return xc * lax.rsqrt(var + NORM_EPS) * g.astype(jnp.float32).reshape(RET_HEADS, RET_HEAD_DIM)

def setup_inputs(seed: int = 0) -> dict:
    key = jax.random.key(seed)
    ks = jax.random.split(key, 20)
    f32 = jnp.float32
    nrm = lambda k, shape, s: (jax.random.normal(k, shape, f32) * s)
    return {
        "x": nrm(ks[0], (BATCH, SEQ, D_MODEL), 1.0),
        "meta_tokens": nrm(ks[1], (N_META, D_MODEL), 1.0),
        "norm_mix_g": 1.0 + nrm(ks[2], (DEPTH, D_MODEL), 0.05),
        "w_in": nrm(ks[3], (DEPTH, D_MODEL, IN_WIDTH), D_MODEL ** -0.5),
        "q_norm_g": 1.0 + nrm(ks[4], (DEPTH, ATTN_HEAD_DIM), 0.05),
        "k_norm_g": 1.0 + nrm(ks[5], (DEPTH, ATTN_HEAD_DIM), 0.05),
        "attn_sinks": nrm(ks[6], (DEPTH, ATTN_HEADS), 0.5),
        "attn_out_g": 1.0 + nrm(ks[7], (DEPTH, ATTN_WIDTH), 0.05),
        "ret_norm_g": 1.0 + nrm(ks[8], (DEPTH, RET_WIDTH), 0.05),
        "w_out": nrm(ks[9], (DEPTH, MIX_WIDTH, D_MODEL), 0.5 * MIX_WIDTH ** -0.5),
        "norm_ffn_g": 1.0 + nrm(ks[10], (DEPTH, D_MODEL), 0.05),
        "router_w": nrm(ks[11], (DEPTH, D_MODEL, N_EXPERTS), D_MODEL ** -0.5),
        "router_b": nrm(ks[12], (DEPTH, N_EXPERTS), 0.01),
        "w_gate_up": nrm(ks[13], (DEPTH, N_EXPERTS, D_MODEL, 2 * D_FF), D_MODEL ** -0.5),
        "b_gate_up": nrm(ks[14], (DEPTH, N_EXPERTS, 2 * D_FF), 0.01),
        "w_down": nrm(ks[15], (DEPTH, N_EXPERTS, D_FF, D_MODEL), 0.5 * D_FF ** -0.5),
        "b_down": nrm(ks[16], (DEPTH, N_EXPERTS, D_MODEL), 0.01),
    }

def reference(x, meta_tokens, norm_mix_g, w_in, q_norm_g, k_norm_g, attn_sinks, attn_out_g,
              ret_norm_g, w_out, norm_ffn_g, router_w, router_b, w_gate_up, b_gate_up, w_down, b_down):
    dt = x.dtype
    B = x.shape[0]
    pad = jnp.zeros((B, META_PAD, D_MODEL), dt)
    meta = jnp.broadcast_to(meta_tokens.astype(dt)[None], (B, N_META, D_MODEL))
    h = jnp.concatenate([pad, meta, x], axis=1)
    L = h.shape[1]
    key_mask = (jnp.arange(L) >= META_PAD).astype(jnp.float32)[None, :, None, None]
    o_qa, o_ka, o_va = 0, ATTN_WIDTH, ATTN_WIDTH + KV_WIDTH
    o_qr = ATTN_WIDTH + 2 * KV_WIDTH
    o_kr, o_vr, o_gr = o_qr + RET_WIDTH, o_qr + 2 * RET_WIDTH, o_qr + 3 * RET_WIDTH

    for layer in range(DEPTH):
        xn = _rms_norm(h, norm_mix_g[layer]).astype(dt)
        proj = xn @ w_in[layer]
        q_a = proj[..., o_qa:o_ka].reshape(B, L, ATTN_HEADS, ATTN_HEAD_DIM)
        k_a = proj[..., o_ka:o_va].reshape(B, L, ATTN_KV_HEADS, ATTN_HEAD_DIM)
        v_a = proj[..., o_va:o_qr].reshape(B, L, ATTN_KV_HEADS, ATTN_HEAD_DIM)
        q_r = proj[..., o_qr:o_kr].astype(jnp.float32).reshape(B, L, RET_HEADS, RET_HEAD_DIM)
        k_r = proj[..., o_kr:o_vr].astype(jnp.float32).reshape(B, L, RET_HEADS, RET_HEAD_DIM)
        v_r = proj[..., o_vr:o_gr].astype(jnp.float32).reshape(B, L, RET_HEADS, RET_HEAD_DIM)
        g_r = proj[..., o_gr:].astype(jnp.float32)
        k_r = k_r * (RET_HEAD_DIM ** -0.5) * key_mask

        attn = _swa_sink_attention(q_a, k_a, v_a, q_norm_g[layer], k_norm_g[layer], attn_sinks[layer])
        attn = _rms_norm(attn.reshape(B, L, ATTN_HEADS, ATTN_HEAD_DIM),
                         attn_out_g[layer].reshape(ATTN_HEADS, ATTN_HEAD_DIM)).reshape(B, L, ATTN_WIDTH)
        ret = _group_norm_heads(_retention(q_r, k_r, v_r), ret_norm_g[layer]).reshape(B, L, RET_WIDTH)
        ret = ret * jax.nn.silu(g_r)

        mixed = jnp.concatenate([attn, ret], axis=-1).astype(dt) @ w_out[layer]
        h = h + mixed.astype(dt)

        xf = _rms_norm(h, norm_ffn_g[layer]).astype(dt).reshape(B * L, D_MODEL)
        logits = xf.astype(jnp.float32) @ router_w[layer].astype(jnp.float32) + router_b[layer].astype(jnp.float32)
        top_vals, top_idx = lax.top_k(logits, TOP_K)
        gate_w = jax.nn.softmax(top_vals, axis=-1)
        combine = jnp.einsum('tk,tke->te', gate_w, jax.nn.one_hot(top_idx, N_EXPERTS, dtype=jnp.float32))
        moe = jnp.zeros((B * L, D_MODEL), jnp.float32)
        for e in range(N_EXPERTS):
            gu = xf @ w_gate_up[layer, e] + b_gate_up[layer, e]
            gate = jnp.minimum(gu[:, :D_FF], SWIGLU_LIMIT)
            up = jnp.clip(gu[:, D_FF:], -SWIGLU_LIMIT, SWIGLU_LIMIT)
            y = ((up + 1.0) * gate * jax.nn.sigmoid(SWIGLU_ALPHA * gate)) @ w_down[layer, e] + b_down[layer, e]
            moe = moe + combine[:, e:e + 1] * y.astype(jnp.float32)
        h = h + moe.reshape(B, L, D_MODEL).astype(dt)

    return h[:, CHUNK:]


_drawn_inputs = setup_inputs


def setup_inputs(seed=0):
    import zlib

    import numpy as np

    out = dict(_drawn_inputs(seed))
    spreads = {}
    factors = {'attn_sinks': 64.0,
     'ret_norm_g': 3.329,
     'router_b': 11.629,
     'b_gate_up': 23.5,
     'b_down': 8.0,
     'q_norm_g': 2.968,
     'k_norm_g': 2.901,
     'attn_out_g': 2.759}
    for name, (base, spread) in spreads.items():
        noise = np.random.default_rng([zlib.crc32(name.encode()), seed]).standard_normal(out[name].shape)
        drawn = base * np.exp(spread * noise) if base else spread * noise
        out[name] = __import__('jax').numpy.asarray(drawn.astype(out[name].dtype))
    for name, factor in factors.items():
        out[name] = (out[name] * factor).astype(out[name].dtype)
    return out
```

```python
from contextlib import ExitStack

import numpy as np
import concourse.bass as bass
from concourse import mybir

F32 = mybir.dt.float32
BF16 = mybir.dt.bfloat16
I32 = mybir.dt.int32
ALU = mybir.AluOpType
ACT = mybir.ActivationFunctionType
X = mybir.AxisListType.X

P = 128
D = 1024
KT = D // P
SEQ = 256
NT = SEQ // P
META = 16
CHUNK = 64
META_POS = CHUNK - META
KEYS = META + SEQ
HEADS, KV_HEADS, HD = 8, 2, 64
RH, RD = 4, 128
E = 32
CAP = 64
FF = 1024
LIMIT, ALPHA = 7.0, 1.702
EPS = 1e-5
MASKED = -1e32
BIG = 3e38

SLOT = 2048
NSLOT = 16
EARLY = 12
EC = 12
UNROLL = 4
GROUPS = E // UNROLL
TURNS = UNROLL * EC // NSLOT

PROJ = [("kv", 512, 256, True), ("qa", 0, 512, False), ("kr", 1280, 512, True),
        ("qr", 768, 512, False), ("vr", 1792, 512, True), ("gr", 2304, 512, False)]
KV, QA, KR, QR, VR, GR = range(6)
IN_CHUNKS = [(g, k, SLOT // p[2]) for g, p in enumerate(PROJ) for k in range(0, KT, SLOT // p[2])]
GROUP_END = [sum(1 for c in IN_CHUNKS if c[0] <= g) for g in range(len(PROJ))]
PRE = len(IN_CHUNKS) + 4
BASE = PRE - EARLY

TAB = {}
for _name, _n in (("ident", P), ("tri", P), ("iota1", P), ("expert", E + 1), ("g_mix", KT), ("g_ffn", KT),
                  ("g_out", KT), ("g_q", 1), ("g_k", 1), ("sinks", HEADS), ("slope", HEADS), ("br", E), ("wr", KT * E)):
    TAB[_name] = (sum(n for _, n in TAB.values()), _n)
TAB_W = sum(n for _, n in TAB.values())
MIX_W = NT * KEYS + RH * SEQ + SEQ


def pre_slot(c):
    return c % EARLY


def moe_slot(n):
    return (BASE + n) % NSLOT


def moe_turn(n):
    s = moe_slot(n)
    before = sum(1 for c in range(PRE) if pre_slot(c) == s)
    return before + (BASE + n) // NSLOT - (1 if s < BASE else 0)


def mixer_table():
    qpos = CHUNK + np.arange(SEQ)
    kpos = np.concatenate([META_POS + np.arange(META), qpos])
    seen = np.zeros((SEQ, KEYS), bool)
    seen[:, :META] = True
    gap = qpos[:, None] // CHUNK - kpos[None, :] // CHUNK
    seen |= (gap >= 0) & (gap <= 1)
    dist = np.where(seen, -np.abs(qpos[:, None] - kpos[None, :]).astype(np.float64), MASKED)
    log_g = np.log1p(-(2.0 ** (-5.0 - np.arange(RH))))
    delta = qpos[None, :] - kpos[:, None]
    decay = np.where(delta >= 0, np.exp(log_g[:, None, None] * np.maximum(delta, 0)), 0.0) * RD ** -0.5
    meta = np.zeros((P, SEQ))
    for j in range(RH):
        meta[32 * j:32 * j + META] = decay[j, :META]
    return np.concatenate([dist.reshape(NT, P, KEYS).transpose(1, 0, 2).reshape(P, -1),
                           decay[:, META:META + P].transpose(1, 0, 2).reshape(P, -1), meta], 1).astype(np.float32)


def small_table(v):
    def cols(a, n):
        return a.reshape(n, P).T

    def rows(a):
        return np.broadcast_to(a.reshape(1, -1), (P, a.size))

    f = np.float32
    t = dict(
        ident=np.eye(P, dtype=f), tri=(np.arange(P)[:, None] < np.arange(P)[None, :]).astype(f),
        iota1=rows((np.arange(P) % CAP + 1).astype(f)),
        expert=((np.arange(P)[:, None] % E) == (np.arange(E + 1)[None, :] % E)).astype(f),
        g_mix=cols(v["norm_mix_g"], KT), g_ffn=cols(v["norm_ffn_g"], KT),
        g_out=np.concatenate([cols(v["attn_out_g"], KT // 2), cols(v["ret_norm_g"], KT // 2)], 1),
        g_q=np.tile(v["q_norm_g"][0], 2)[:, None], g_k=np.tile(v["k_norm_g"][0], 2)[:, None],
        sinks=rows(v["attn_sinks"]), slope=rows((2.0 ** (-8.0 * np.arange(1, HEADS + 1) / HEADS)).astype(f)),
        br=rows(v["router_b"]), wr=v["router_w"][0].reshape(KT, P, E).transpose(1, 0, 2).reshape(P, -1))
    return np.ascontiguousarray(np.concatenate([t[k] for k in TAB], 1))


def build(nc, a):
    ctx = ExitStack()
    with ctx:
        def sb(name, shape, dt=F32):
            return ctx.enter_context(nc.sbuf_tensor(name, shape, dt))

        def sem(name):
            return ctx.enter_context(nc.semaphore(name))

        ring = sb("ring", [P, NSLOT * SLOT])
        h = sb("h", [P, NT, D])
        xr = sb("xr", [P, NT, D])
        xT = sb("xT", [P, KT, KEYS])
        table = sb("table", [P, TAB_W])
        ones = sb("ones", [P, P])
        bias = sb("bias", [96, 2 * FF], BF16)
        bdown = sb("bdown", [E, D])
        half = sb("half", [P, 16])
        rank = sb("rank", [P, NT, E + 1])
        gatew = sb("gatew", [P, NT, E + 1])
        rounds_i = sb("rounds_i", [1, 1], I32)
        va = sb("va", [P, NT, P])
        vam = sb("vam", [META, P])
        lx = sb("lx", [P, NT, E + 8])
        lrep = sb("lrep", [P, NT, E + 8])
        mask = sb("mask", [P, NT, E])
        eexp = sb("eexp", [P, NT, E])
        gT = sb("gT", [E, NT, P])
        small = sb("small", [P, 160])
        area = sb("area", [P, 9216])

        def tab(name):
            c0, n = TAB[name]
            return table[:, c0:c0 + n]

        ident, tri, iota1, expert = tab("ident"), tab("tri"), tab("iota1"), tab("expert")
        g_mix, g_ffn, g_out, slope, sinks = tab("g_mix"), tab("g_ffn"), tab("g_out"), tab("slope"), tab("sinks")
        wr = tab("wr").rearrange("p (k e) -> p k e", k=KT)

        class Views:
            def __init__(self, tensor, start, end):
                self.t, self.at, self.end = tensor, start, end

            def take(self, parts, *shape, dt=F32):
                n = int(np.prod(shape)) * (2 if dt == BF16 else 4) // 4
                v = self.t[0:parts, self.at:self.at + n]
                self.at += n
                assert self.at <= self.end, (self.at, self.end)
                if dt != F32:
                    v = v.bitcast(dt)
                if len(shape) == 2:
                    v = v.rearrange("p (a b) -> p a b", a=shape[0])
                if len(shape) == 3:
                    v = v.rearrange("p (a b c) -> p a b c", a=shape[0], b=shape[1])
                return v

        m = Views(area, 0, 9216)
        nat_q = m.take(P, NT, 512)
        nat_k = m.take(P, NT, 512)
        krm = m.take(P, RD)
        vrm = m.take(P, RD)
        vr = m.take(P, NT, 512)
        gr = m.take(P, NT, 512)
        qaT = m.take(P, 4, SEQ)
        kaT = m.take(P, KV_HEADS, KEYS)
        qrT = m.take(P, RH, SEQ)
        krT = m.take(P, RH, KEYS)
        ka = vr[:, :, 0:P]
        kn = vr[:, :, P:P + 256]
        kam = vrm[0:64, 0:HD]
        knm = krT.rearrange("p a b -> p (a b)")[0:64, 0:P]
        xm = qrT.rearrange("p a b -> p (a b)")
        osq = nat_k[:, 0, :]
        m = Views(area, 0, 9216)
        xs = [m.take(P, NT, D, dt=BF16) for _ in range(3)]
        sel = [m.take(P, NT, CAP, dt=BF16) for _ in range(2)]
        gsel = [m.take(P, NT, P) for _ in range(2)]
        selT = [m.take(P, NT, P) for _ in range(2)]
        xg = [m.take(P, KT, CAP) for _ in range(2)]
        pick = [m.take(96, CAP, dt=BF16) for _ in range(2)]
        gate = m.take(P, 512)
        sig = m.take(P, 512)
        up = m.take(P, 512)
        act_o = m.take(P, 512)
        actT = m.take(P, 4, P)
        y = m.take(P, 512)
        m = Views(ring, EARLY * SLOT, NSLOT * SLOT)
        mixer_table_sb = ring[:, m.at:m.at + MIX_W]
        dist = m.take(P, NT, KEYS)
        decay = m.take(P, RH, SEQ)
        decaym = m.take(P, SEQ)
        prob = [m.take(P, HEADS, META + P), m.take(P, HEADS, KEYS)]
        at = m.at
        pT = m.take(P, 4, 3, P)
        attT = [m.take(P, 384) for _ in range(2)]
        attm = m.take(P, SEQ)
        m.at = at
        bstage = m.take(96, 2 * FF)
        bhigh = m.take(96, FF // 2)
        sqk = prob[1].rearrange("p a b -> p (a b)")

        bank = [ctx.enter_context(nc.psum_tensor(f"bank{i}", [P, 512], F32)) for i in range(8)]

        cols = [0]

        def col(n):
            cols[0] += n
            assert cols[0] <= 160
            return small[:, cols[0] - n:cols[0]]

        ssx, ssk, ssq = col(3), col(5), col(16)
        mx, negm, rsum, esink = ([col(HEADS) for _ in range(NT)] for _ in range(4))
        ssa, stats, mv, sso = col(HEADS), col(6), col(2 * NT * RH), col(NT)
        top8, rep8, nmax, den, over = col(8), col(8), col(NT), col(NT), col(5)

        slot_full = [sem(f"slot_full{s}") for s in range(NSLOT)]
        chunk_used = sem("chunk_used")
        ld_xT, ld_x, ld_tab, ld_mix, ld_bias, ld_bdown = (
            sem(f"loaded_{n}") for n in ("xT", "x", "table", "mixer_table", "bias", "bdown"))
        stored = sem("stored")
        dv = sem("dve_chain")
        pc = sem("pool_chain")
        ones_set, half_set = sem("ones_set"), sem("half_set")
        xg_gain = sem("x_times_gain")
        sq_done, var_ready, rstd_ready = sem("squares_summed"), sem("var_ready"), sem("rstd_ready")
        proj_sb = sem("proj_sb")
        bias_parts = sem("bias_parts")
        kn_ready, qn_ready = sem("kn_ready"), sem("qn_ready")
        qkT_ps, qkT_sb = sem("qkT_ps"), sem("qkT_sb")
        rT_ps, rT_sb = sem("rT_ps"), sem("rT_sb")
        score_ps, score_sb = sem("score_ps"), sem("score_sb")
        max_ready, exp_done = sem("max_ready"), sem("exp_done")
        pT_ps, pT_sb = sem("pT_ps"), sem("pT_sb")
        pv_ps, pv_sb = sem("pv_ps"), sem("pv_sb")
        att_ps, att_sb = sem("att_ps"), sem("att_sb")
        ret_ps = sem("ret_ps")
        gate_sig = sem("gate_sigmoid")
        mix_ready, mixT_ps, mixT_sb = sem("mix_ready"), sem("mixT_ps"), sem("mixT_sb")
        out_ps, h_ready = sem("out_ps"), sem("h_ready")
        xf_ready, xfT_ps, xfT_sb = sem("xf_ready"), sem("xfT_ps"), sem("xfT_sb")
        high_sb, low_ready = sem("high_part"), sem("rest_ready")
        logit_ps, nmax_ready, e_exp = sem("logit_ps"), sem("nmax_ready"), sem("gate_exp")
        mask_ready, rank_ps, rounds_ready = sem("mask_ready"), sem("rank_ps"), sem("rounds_ready")
        gatew_ready, gT_ps, gT_sb, bd_ps, bd_sb = (sem(n) for n in ("gatew_ready", "gT_ps", "gT_sb", "bdown_ps", "bdown_added"))
        sel_ready, gsel_ready, pick_ready = sem("sel_ready"), sem("gsel_ready"), sem("pick_ready")
        xg_ps, xg_sb = sem("xg_ps"), sem("xg_sb")
        gate_sb, sig_sb, act_sb = sem("gate_sb"), sem("sig_sb"), sem("act_sb")
        selT_ps, selT_sb = sem("selT_ps"), sem("selT_sb")
        actT_ps, actT_sb = sem("actT_ps"), sem("actT_sb")
        y_sb = sem("y_sb")
        add_ps, add_sb = sem("add_ps"), sem("add_sb")

        def ret_bank(t, hd):
            return bank[((3, 5), (2, 6))[t][hd // 2]][:, (hd % 2) * RD:(hd % 2 + 1) * RD]

        block = ctx.enter_context(nc.Block())

        def slot(s):
            return ring[:, s * SLOT:(s + 1) * SLOT]

        def tok(t):
            return slice(META + t * P, META + (t + 1) * P)

        def four(ap):
            return ap.rearrange("p (a b) -> p a b", a=4)

        @block.sync
        def _(sp):
            w_in = a["w_in"][0].rearrange("(k p) n -> p k n", p=P)

            def load_in(c):
                g, k, n = IN_CHUNKS[c]
                _, c0, w, _ = PROJ[g]
                sp.dma_start(slot(pre_slot(c)).rearrange("p (k n) -> p k n", n=w),
                             w_in[:, k:k + n, c0:c0 + w]).then_inc(slot_full[pre_slot(c)], 16)

            sp.dma_start(table[:], a["small_table"]).then_inc(ld_tab, 16)
            sp.dma_start(xT[:], a["xT"]).then_inc(ld_xT, 16)
            load_in(0)
            sp.dma_start(h[:], a["x"].rearrange("(t p) d -> p t d", p=P)).then_inc(ld_x, 16)
            for j in range(4):
                sp.dma_start(xm[32 * j:32 * j + 32, :], a["x_first"]).then_inc(ld_x, 16)
            load_in(1)
            load_in(2)
            for j in range(3):
                sp.dma_start(bstage[32 * j:32 * j + 32, :], a["b_gate_up"][0]).then_inc(ld_bias, 16)
            load_in(3)
            sp.dma_start(mixer_table_sb, a["mixer_table"]).then_inc(ld_mix, 16)
            for c in range(4, len(IN_CHUNKS)):
                load_in(c)
            sp.dma_start(bdown[:], a["b_down"][0]).then_inc(ld_bdown, 16)
            w_out = a["w_out"][0].rearrange("(c i p) n -> c p i n", p=P, i=2)
            for j in range(4):
                c = len(IN_CHUNKS) + j
                if c >= EARLY:
                    sp.wait_ge(chunk_used, c - EARLY + 1)
                sp.dma_start(slot(pre_slot(c)).rearrange("p (i n) -> p i n", i=2),
                             w_out[j]).then_inc(slot_full[pre_slot(c)], 16)

            gu = a["w_gate_up"][0].rearrange("e (k p) n -> e k p n", p=P)
            dn = a["w_down"][0].rearrange("e (j p i) n -> e j p (i n)", p=P, i=2)

            def load_group(g, it, first):
                for n in range(UNROLL * EC):
                    u, c = divmod(n, EC)
                    s = moe_slot(n)
                    if first and n + BASE < NSLOT:
                        if s < EARLY:
                            sp.wait_ge(chunk_used, s + 1)
                        elif s == EARLY:
                            sp.wait_ge(ret_ps, RH)
                            sp.wait_ge(pv_ps, 2 * NT)
                    elif first:
                        q = n + BASE - NSLOT
                        sp.wait_ge(chunk_used, EARLY + q + 1 if q < BASE else PRE + q - BASE + 1)
                    else:
                        sp.wait_ge(chunk_used, it * (UNROLL * EC) + (PRE + n - NSLOT + 1))
                    src = (gu[bass.ds(g * UNROLL + u, 1), c] if c < KT else dn[bass.ds(g * UNROLL + u, 1), c - KT])
                    sp.dma_start(slot(s), src.rearrange("e p n -> (e p) n")).then_inc(slot_full[s], 16)

            load_group(0, 0, True)
            with sp.Fori(1, GROUPS) as g:
                load_group(g, g, False)
            sp.wait_ge(rounds_ready, 1)
            rounds = sp.value_load(rounds_i[0:1, 0:1], min_val=1, max_val=SEQ // CAP)
            with sp.If(rounds > 1):
                with sp.Fori(1, rounds) as r:
                    with sp.Fori(0, GROUPS) as g:
                        load_group(g, r * GROUPS + g, False)
            for t in range(NT):
                sp.wait_ge(add_sb, rounds * (NT * E) + (t + 2))
                sp.dma_start(a["out"][0, t * P:(t + 1) * P, :], h[:, t, :]).then_inc(stored, 16)
            sp.wait_ge(stored, 16 * NT)

        @block.gpsimd
        def _(pool):
            G = nc.gpsimd
            G.memset(half[:], -0.5).then_inc(half_set, 1)
            G.memset(ones[:], 1.0).then_inc(ones_set, 1)
            pool.wait_ge(half_set, 1)
            done = [0]

            def power(*vs):
                for v in vs:
                    done[0] += 1
                    pool.wait_ge(var_ready, done[0])
                    G.tensor_tensor(v, v, half[0:v.shape[0], 0:v.shape[1]], ALU.pow).then_inc(rstd_ready, 1)

            power(ssx[:], ssk[:, 0:4], ssk[0:64, 4:5], ssq[:])
            pool.wait_ge(ld_bias, 48)
            steps = [0]

            def link(ins):
                steps[0] += 1
                ins.then_inc(pc, 1)
                pool.wait_ge(pc, steps[0])

            link(G.tensor_copy(bias[0:32, :], bstage[0:32, :]))
            hw = FF
            bh = bhigh.bitcast(BF16)
            for r, times in ((32, 1), (64, 2)):
                rows = slice(r, r + 32)
                for c in range(0, 2 * FF, hw):
                    cs = slice(c, c + hw)
                    for _ in range(times):
                        link(G.tensor_copy(bh[rows, :], bstage[rows, cs]))
                        link(G.tensor_tensor(bstage[rows, cs], bstage[rows, cs], bh[rows, :], ALU.subtract))
                    link(G.tensor_copy(bias[rows, cs], bstage[rows, cs]))
            G.memset(bh[0:1, 0:2], 0.0).then_inc(bias_parts, 1)
            power(*([ssa[:]] * NT), *[mv[:, 2 * RH * t + 1:2 * RH * (t + 1):2] for t in range(NT)],
                  *[sso[:, t:t + 1] for t in range(NT)])

        @block.scalar
        def _(act):
            S = nc.scalar
            act.wait_ge(ld_x, 16 * 5)
            for t in range(NT):
                S.activation(xr[:, t, :], h[:, t, :], ACT.Square, accum_out=ssx[:, t:t + 1])
            S.activation(vr.rearrange("p a b -> p (a b)"), xm, ACT.Square, accum_out=ssx[:, 2:3]).then_inc(sq_done, 1)
            act.wait_ge(rstd_ready, 1)

            def take(g):
                act.wait_ge(chunk_used, GROUP_END[g])
                for t in range(NT):
                    src = bank[2 * (g % 2) + t]
                    if g == KV:
                        S.activation(ka[:, t, :], src[:, 0:P], ACT.Copy, scale=ssx[:, t:t + 1])
                        last = S.activation(va[:, t, :], src[:, P:2 * P], ACT.Copy, scale=ssx[:, t:t + 1])
                    else:
                        dst = {QA: nat_q, QR: nat_q, KR: nat_k, VR: vr, GR: gr}[g]
                        last = S.activation(dst[:, t, :], src[:], ACT.Copy, scale=ssx[:, t:t + 1])
                if g == KV:
                    S.activation(kam, bank[4][0:64, 0:HD], ACT.Copy, scale=ssx[0:64, 2:3])
                    for j in range(KV_HEADS):
                        r0 = 64 + 32 * j
                        last = S.activation(vam[:, j * HD:(j + 1) * HD], bank[4][r0:r0 + META, 0:HD], ACT.Copy,
                                            scale=ssx[0:META, 2:3])
                elif g in (KR, VR):
                    last = S.activation({KR: krm, VR: vrm}[g], bank[4][:, 0:RD], ACT.Copy, scale=ssx[:, 2:3])
                last.then_inc(proj_sb, 1)

            def softmax_exp(t):
                act.wait_ge(max_ready, t + 1)
                for hd in range(HEADS):
                    S.activation(prob[t][:, hd, :], prob[t][:, hd, :], ACT.Exp, bias=negm[t][:, hd:hd + 1],
                                 accum_out=rsum[t][:, hd:hd + 1])
                S.activation(esink[t], esink[t], ACT.Exp).then_inc(exp_done, 1)

            def take_rT(i):
                act.wait_ge(rT_ps, i + 1)
                src = bank[(5, 6, 7, 7, 5)[i]]
                if i == 2:
                    S.copy(krT[:, :, 0:META], four(src[:, 0:P])[:, :, 0:META]).then_inc(rT_sb, 1)
                elif i < 2:
                    S.copy(krT[:, :, tok(i)], four(src[:])).then_inc(rT_sb, 1)
                else:
                    S.copy(qrT[:, :, (i - 3) * P:(i - 2) * P], four(src[:])).then_inc(rT_sb, 1)

            def take_pT(t, q):
                act.wait_ge(pT_ps, 2 * t + q + 1)
                S.copy(pT[0:META, :, 0, :], four(bank[5][0:META, :]))
                last = S.copy(pT[:, :, 1, :], four(bank[6][:]))
                if t:
                    last = S.copy(pT[:, :, 2, :], four(bank[7][:]))
                last.then_inc(pT_sb, 1)

            take(KV)
            take(QA)
            act.wait_ge(qkT_ps, 2)
            take(KR)
            softmax_exp(0)
            softmax_exp(1)
            for i in range(3):
                take_rT(i)
            act.wait_ge(qkT_ps, 4)
            take(QR)
            act.wait_ge(bias_parts, 1)
            take_rT(3)
            take_rT(4)
            take_pT(0, 0)
            take(VR)
            act.wait_ge(pv_ps, 1)
            take_pT(0, 1)
            take(GR)
            act.wait_ge(proj_sb, GR + 1)
            for t in range(NT):
                S.activation(xr[:, t, 512:1024], gr[:, t, :], ACT.Sigmoid).then_inc(gate_sig, 1)
            act.wait_ge(pv_ps, 2)
            take_pT(1, 0)
            act.wait_ge(pv_ps, 3)
            take_pT(1, 1)
            for t in range(NT):
                act.wait_ge(h_ready, t + 1)
                S.activation(xr[:, t, :], h[:, t, :], ACT.Square, accum_out=sso[:, t:t + 1]).then_inc(sq_done, 1)
            for t in range(NT):
                act.wait_ge(xf_ready, t + 1)
                S.copy(xs[0][:, t, :], xr[:, t, :]).then_inc(high_sb, 1)
            for t in range(NT):
                act.wait_ge(nmax_ready, t + 1)
                S.activation(eexp[:, t, :], lx[:, t, 0:E], ACT.Exp, bias=nmax[:, t:t + 1]).then_inc(e_exp, 1)
            act.wait_ge(low_ready, NT)
            for t in range(NT):
                S.copy(xs[1][:, t, :], xr[:, t, :]).then_inc(high_sb, 1)
            act.wait_ge(gT_ps, 1)
            S.copy(gT[:], bank[6][0:E, 0:NT * P].rearrange("p (a b) -> p a b", a=NT)).then_inc(gT_sb, 1)

            act.wait_ge(rounds_ready, 1)
            rounds = act.value_load(rounds_i[0:1, 0:1], min_val=1, max_val=SEQ // CAP)
            with act.Fori(0, rounds * GROUPS) as it:
                for u in range(UNROLL):
                    n = it * UNROLL + u
                    act.wait_ge(gate_sb, n + 1)
                    S.activation(sig, gate, ACT.Sigmoid, scale=ALPHA).then_inc(sig_sb, 1)
                    act.wait_ge(selT_ps, n + 1)
                    S.copy(selT[u % 2], bank[5][:, 0:NT * P].rearrange("p (a b) -> p a b", a=NT)).then_inc(selT_sb, 1)
                    act.wait_ge(actT_ps, n + 1)
                    S.copy(actT, four(bank[3][:])).then_inc(actT_sb, 1)
                    act.wait_ge(chunk_used, it * (UNROLL * EC) + (PRE + (u + 1) * EC))
                    S.copy(y, bank[2][:]).then_inc(y_sb, 1)

        @block.vector
        def _(dve):
            cnt = [0]
            var = [0]
            V = nc.vector

            def link(ins):
                cnt[0] += 1
                ins.then_inc(dv, 1)
                dve.wait_ge(dv, cnt[0])

            def variance(v, n):
                V.tensor_scalar(v, v, 1.0 / n, EPS, ALU.mult, ALU.add).then_inc(var_ready, 1)
                var[0] += 1

            def rstd_wait(behind=0):
                dve.wait_ge(rstd_ready, var[0] - behind)

            def spread_cols(ap, n, w):
                return ap.unsqueeze(2).broadcast_to([ap.shape[0], n, w])

            dve.wait_ge(ld_tab, 16)
            dve.wait_ge(ld_xT, 16)
            for k in range(0, KT, 2):
                V.tensor_tensor(xT[:, k:k + 2, :], xT[:, k:k + 2, :], spread_cols(g_mix[:, k:k + 2], 2, KEYS), ALU.mult).then_inc(xg_gain, 1)
            dve.wait_ge(sq_done, 1)
            variance(ssx[:], D)
            dve.wait_ge(proj_sb, 1)
            sk = sqk[:, 0:256]
            link(V.tensor_tensor(sk.rearrange("p (a b) -> p a b", a=NT), ka, ka, ALU.mult))
            link(V.tensor_reduce(ssk[:, 0:4], four(sk), X, ALU.add))
            variance(ssk[:, 0:4], HD)
            link(V.tensor_tensor(sqk[0:64, 256:320], kam, kam, ALU.mult))
            link(V.tensor_reduce(ssk[0:64, 4:5], sqk[0:64, 256:320], X, ALU.add))
            variance(ssk[0:64, 4:5], HD)
            rstd_wait(1)
            for t in range(NT):
                for g in range(KV_HEADS):
                    link(V.tensor_scalar(kn[:, t, g * P:(g + 1) * P].rearrange("p (a b) -> p a b", a=2),
                                         ka[:, t, g * HD:(g + 1) * HD].unsqueeze(1).broadcast_to([P, 2, HD]),
                                         ssk[:, 2 * t + g:2 * t + g + 1], None, ALU.mult))
            rstd_wait()
            V.tensor_scalar(knm.rearrange("p (a b) -> p a b", a=2), kam.unsqueeze(1).broadcast_to([64, 2, HD]),
                            ssk[0:64, 4:5], None, ALU.mult).then_inc(kn_ready, 1)
            dve.wait_ge(qkT_ps, 1)
            V.tensor_scalar(kaT[:, :, META:KEYS], bank[5][:].rearrange("p (a b) -> p a b", a=2),
                            tab("g_k"), None, ALU.mult).then_inc(qkT_sb, 1)
            dve.wait_ge(qkT_ps, 2)
            V.tensor_scalar(kaT[:, :, 0:META], bank[6][:, 0:64].rearrange("p (a b) -> p a b", a=2)[:, :, 0:META],
                            tab("g_k"), None, ALU.mult).then_inc(qkT_sb, 1)
            dve.wait_ge(proj_sb, 2)
            sq = sqk[:, 0:1024]
            link(V.tensor_tensor(sq.rearrange("p (a b) -> p a b", a=NT), nat_q, nat_q, ALU.mult))
            link(V.tensor_reduce(ssq[:], sq.rearrange("p (a b) -> p a b", a=16), X, ALU.add))
            variance(ssq[:], HD)
            rstd_wait()
            nq = nat_q.rearrange("p t (a b) -> p (t a) b", b=HD)
            V.tensor_tensor(nq, nq, spread_cols(ssq, 16, HD), ALU.mult).then_inc(qn_ready, 1)
            for t in range(NT):
                dve.wait_ge(qkT_ps, 3 + t)
                V.tensor_scalar(qaT[:, :, t * P:(t + 1) * P], four(bank[(7, 5)[t]][:]),
                                tab("g_q"), HD ** -0.5, ALU.mult, ALU.mult).then_inc(qkT_sb, 1)
            dve.wait_ge(ld_mix, 16)
            for t in range(NT):
                nk = META + P * (t + 1)
                for hd in range(HEADS):
                    i = t * HEADS + hd
                    dve.wait_ge(score_ps, i + 1)
                    V.scalar_tensor_tensor(prob[t][:, hd, :], dist[:, t, 0:nk], slope[:, hd:hd + 1], bank[5 + (i + 1) % 3][:, 0:nk],
                                           ALU.mult, ALU.add).then_inc(score_sb, 1)
                dve.wait_ge(score_sb, HEADS * (t + 1))
                link(V.tensor_reduce(mx[t], prob[t], X, ALU.max))
                link(V.tensor_tensor(mx[t], mx[t], sinks, ALU.max))
                link(V.tensor_tensor(esink[t], sinks, mx[t], ALU.subtract))
                V.tensor_scalar(negm[t], mx[t], -1.0, None, ALU.mult).then_inc(max_ready, 1)
            for t in range(NT):
                dve.wait_ge(exp_done, t + 1)
                link(V.tensor_tensor(rsum[t], rsum[t], esink[t], ALU.add))
                link(V.reciprocal(rsum[t], rsum[t]))

            def attention_norm(t):
                dve.wait_ge(pv_ps, 2 * t + 2)
                o = xr[:, t, 0:512].rearrange("p (a b) -> p a b", a=HEADS)
                sqv = osq.rearrange("p (a b) -> p a b", a=HEADS)
                V.tensor_tensor(o, bank[4][:].rearrange("p (a b) -> p a b", a=HEADS), spread_cols(rsum[t], HEADS, HD),
                                ALU.mult).then_inc(pv_sb, 1)
                dve.wait_ge(pv_sb, t + 1)
                link(V.tensor_tensor(sqv, o, o, ALU.mult))
                link(V.tensor_reduce(ssa[:], sqv, X, ALU.add))
                variance(ssa[:], HD)
                rstd_wait()
                V.tensor_tensor(o, o, spread_cols(ssa, HEADS, HD), ALU.mult).then_inc(mix_ready, 1)

            def times_decay(hd):
                dve.wait_ge(att_ps, 2 + hd)
                if hd >= 2:
                    dve.wait_ge(ret_ps, hd - 1)
                src, dst = bank[(hd + 1) % 2], attT[hd % 2]
                V.tensor_tensor(dst[:, 0:256], src[:, 0:256], decay[:, hd, :], ALU.mult)
                V.tensor_tensor(dst[:, 256:384], src[:, 256:384], decay[:, hd, 0:P], ALU.mult).then_inc(att_sb, 1)

            dve.wait_ge(att_ps, 1)
            V.tensor_tensor(attm, bank[0][:, 0:SEQ], decaym, ALU.mult).then_inc(att_sb, 1)
            attention_norm(0)
            times_decay(0)
            times_decay(1)
            dve.wait_ge(gate_sig, NT)
            link(V.tensor_tensor(gr, gr, xr[:, :, 512:1024], ALU.mult))

            def group_stats(hd):
                dve.wait_ge(ret_ps, 2 * (hd // 2) + 2)
                for t in range(NT):
                    o = 2 * (RH * t + hd)
                    link(V.bn_stats(stats[:], ret_bank(t, hd)))
                    link(V.bn_aggr(mv[:, o:o + 2], stats[:]))

            times_decay(2)
            times_decay(3)
            attention_norm(1)
            for hd in range(RH):
                group_stats(hd)
            for t in range(NT):
                V.tensor_scalar(mv[:, 2 * RH * t + 1:2 * RH * (t + 1):2], mv[:, 2 * RH * t + 1:2 * RH * (t + 1):2],
                                1.0, EPS, ALU.mult, ALU.add).then_inc(var_ready, 1)
                var[0] += 1
            for t in range(NT):
                for hd in range(RH):
                    rs = slice(hd * RD, (hd + 1) * RD)
                    o = 2 * (RH * t + hd)
                    link(V.scalar_tensor_tensor(xr[:, t, 512 + hd * RD:512 + (hd + 1) * RD], ret_bank(t, hd), mv[:, o:o + 1],
                                                gr[:, t, rs], ALU.subtract, ALU.mult))
                rstd_wait(1 - t)
                o = xr[:, t, 512:1024].rearrange("p (a b) -> p a b", a=RH)
                V.tensor_tensor(o, o, spread_cols(mv[:, 2 * RH * t + 1:2 * RH * (t + 1):2], RH, RD), ALU.mult).then_inc(mix_ready, 1)
            for i in range(4):
                t, kk = i // 2, 4 * (i % 2)
                dve.wait_ge(mixT_ps, i + 1)
                V.tensor_tensor(xT[:, kk:kk + 4, t * P:(t + 1) * P], four(bank[(0, 1, 5, 6)[i]][:]),
                                spread_cols(g_out[:, kk:kk + 4], 4, P), ALU.mult).then_inc(mixT_sb, 1)
            link(V.memset(lx[:, :, E:E + 8], -BIG))
            link(V.memset(rep8[:], -BIG))
            for t in range(NT):
                if t == 0:
                    dve.wait_ge(out_ps, 1)
                else:
                    dve.wait_ge(chunk_used, PRE)
                for j in range(2):
                    ins = V.tensor_tensor(h[:, t, j * 512:(j + 1) * 512], h[:, t, j * 512:(j + 1) * 512],
                                          bank[(7, 3, 0, 1)[2 * t + j]][:], ALU.add)
                    if j == 0:
                        link(ins)
                ins.then_inc(h_ready, 1)
                dve.wait_ge(sq_done, 2 + t)
                variance(sso[:, t:t + 1], D)
                rstd_wait()
                V.tensor_scalar(xr[:, t, :], h[:, t, :], sso[:, t:t + 1], None, ALU.mult).then_inc(xf_ready, 1)
            for i in range(4):
                t, kk = i // 2, 4 * (i % 2)
                dve.wait_ge(xfT_ps, i + 1)
                V.tensor_tensor(xT[:, kk:kk + 4, t * P:(t + 1) * P], four(bank[(4, 2, 5, 6)[i]][:]),
                                spread_cols(g_ffn[:, kk:kk + 4], 4, P), ALU.mult).then_inc(xfT_sb, 1)
            for t in range(NT):
                dve.wait_ge(logit_ps, t + 1)
                link(V.tensor_tensor(lx[:, t, 0:E], bank[(3, 7)[t]][:, 0:E], tab("br"), ALU.add))
                link(V.max(top8[:], lx[:, t, 0:E]))
                link(V.tensor_copy(rep8[:, 0:4], top8[:, 0:4]))
                V.tensor_scalar(nmax[:, t:t + 1], top8[:, 0:1], -1.0, None, ALU.mult).then_inc(nmax_ready, 1)
                link(V.match_replace(lrep[:, t, :], rep8[:], lx[:, t, :], BIG))
                V.tensor_scalar(mask[:, t, :], lrep[:, t, 0:E], BIG, None, ALU.is_equal).then_inc(mask_ready, 1)
            dve.wait_ge(high_sb, NT)
            for t in range(NT):
                V.tensor_tensor(xr[:, t, :], xr[:, t, :], xs[0][:, t, :], ALU.subtract).then_inc(low_ready, 1)
            dve.wait_ge(mask_ready, NT)
            dve.wait_ge(rank_ps, 1)
            for t in range(NT):
                link(V.scalar_tensor_tensor(rank[:, t, 0:E], bank[1][:, t * E:(t + 1) * E], 1.0, mask[:, t, :], ALU.add, ALU.mult))
            link(V.tensor_scalar(rank[:, :, E:E + 1], rank[:, :, 0:1], float(CAP), None, ALU.subtract))

            def make_sel(e, b):
                for t in range(NT):
                    ins = V.tensor_scalar(sel[b][:, t, :], iota1[:, 0:CAP], rank[:, t, bass.ds(e, 1)], None, ALU.is_equal)
                ins.then_inc(sel_ready, 1)
                V.tensor_copy(pick[b], expert[0:96, bass.ds(e, 1)].broadcast_to([96, CAP])).then_inc(pick_ready, 1)

            def make_gsel(e, b):
                for t in range(NT):
                    ins = V.tensor_scalar(gsel[b][:, t, :], iota1, rank[:, t, bass.ds(e, 1)], gatew[:, t, bass.ds(e, 1)],
                                          ALU.is_equal, ALU.mult)
                ins.then_inc(gsel_ready, 1)

            def take_xg(b):
                V.tensor_tensor(xg[b], bank[4][:].rearrange("p (a b) -> p a b", a=KT), spread_cols(g_ffn, KT, CAP),
                                ALU.mult).then_inc(xg_sb, 1)

            make_sel(0, 0)
            dve.wait_ge(high_sb, 2 * NT)
            for t in range(NT):
                ins = V.tensor_tensor(xs[2][:, t, :], xr[:, t, :], xs[1][:, t, :], ALU.subtract)
                ins.then_inc(low_ready, 1)
            link(V.tensor_reduce(over[:, 3:4], bank[1][:, 2 * E:3 * E], X, ALU.max))
            for j in range(3):
                link(V.tensor_scalar(over[:, j:j + 1], over[:, 3:4], CAP * (j + 1) + 0.5, None, ALU.is_gt))
            link(V.tensor_reduce(over[:, 4:5], over[:, 0:3], X, ALU.add))
            V.tensor_scalar(rounds_i[:], over[0:1, 4:5], 1.0, None, ALU.add).then_inc(rounds_ready, 1)
            dve.wait_ge(e_exp, NT)
            link(V.tensor_tensor(gatew[:, :, 0:E], eexp[:], mask[:], ALU.mult))
            link(V.tensor_reduce(den[:], gatew[:, :, 0:E], X, ALU.add))
            link(V.reciprocal(den[:], den[:]))
            link(V.tensor_tensor(gatew[:, :, 0:E], gatew[:, :, 0:E], spread_cols(den, NT, E), ALU.mult))
            V.tensor_copy(gatew[:, :, E:E + 1], gatew[:, :, 0:1]).then_inc(gatew_ready, 1)
            dve.wait_ge(xg_ps, 1)
            take_xg(0)
            dve.wait_ge(bd_ps, 1)
            for t in range(NT):
                for j in range(2):
                    V.tensor_tensor(h[:, t, j * 512:(j + 1) * 512], h[:, t, j * 512:(j + 1) * 512],
                                    bank[(2, 3, 6, 7)[2 * t + j]][:], ALU.add).then_inc(bd_sb, 1)
            V.memset(selT[1], 0.0).then_inc(selT_sb, 1)
            V.memset(y, 0.0).then_inc(y_sb, 1)
            V.memset(act_o[:, 0:1], 0.0).then_inc(act_sb, 1)
            V.memset(over[:, 0:1], 0.0).then_inc(add_sb, 1)
            for ready, value in ((bd_sb, 4), (selT_sb, 1), (y_sb, 1), (act_sb, 1), (add_sb, 1)):
                dve.wait_ge(ready, value)

            rounds = dve.value_load(rounds_i[0:1, 0:1], min_val=1, max_val=SEQ // CAP)
            CH = 4
            with dve.Fori(0, rounds) as r:
                with dve.Fori(0, GROUPS) as g:
                    for u in range(UNROLL):
                        n = (r * GROUPS + g) * UNROLL + u
                        e = g * UNROLL + u
                        loc = [0]

                        def step(ins):
                            loc[0] += 1
                            ins.then_inc(dv, 1)
                            dve.wait_ge(dv, n * CH + r + (cnt[0] + loc[0]))

                        make_sel(e + 1, (u + 1) % 2)
                        make_gsel(e, u % 2)
                        dve.wait_ge(chunk_used, (r * GROUPS + g) * (UNROLL * EC) + (PRE + u * EC + KT))
                        V.tensor_scalar(gate, bank[0][:], LIMIT, None, ALU.min).then_inc(gate_sb, 1)
                        step(V.tensor_scalar(up, bank[1][:], LIMIT, -LIMIT, ALU.min, ALU.max))
                        dve.wait_ge(gate_sb, n + 1)
                        step(V.scalar_tensor_tensor(up, up, 1.0, gate, ALU.add, ALU.mult))
                        dve.wait_ge(sig_sb, n + 1)
                        V.tensor_tensor(act_o, up, sig, ALU.mult).then_inc(act_sb, 1)
                        for t in range(NT):
                            dve.wait_ge(add_ps, (n * NT) + (t + 1))
                            for j in range(2):
                                o = h[:, t, j * 512:(j + 1) * 512]
                                ins = V.tensor_tensor(o, o, bank[6 + j][:], ALU.add)
                                if j == 0:
                                    step(ins)
                            ins.then_inc(add_sb, 1)
                        dve.wait_ge(add_sb, n * NT + (NT + 1))
                        dve.wait_ge(xg_ps, n + 2)
                        take_xg((u + 1) % 2)
                        assert loc[0] == CH
                V.tensor_scalar(rank[:], rank[:], float(CAP), None, ALU.subtract).then_inc(dv, 1)
                dve.wait_ge(dv, r * (E * CH + 1) + (E * CH + 1 + cnt[0]))
            for t in range(NT):
                dve.wait_ge(add_ps, rounds * (E * NT) + (t + 1))
                for j in range(2):
                    o = h[:, t, j * 512:(j + 1) * 512]
                    ins = V.tensor_tensor(o, o, bank[6 + j][:], ALU.add)
                    if j == 0:
                        ins.then_inc(bd_sb, 1)
                        dve.wait_ge(bd_sb, 5 + t)
                ins.then_inc(add_sb, 1)

        @block.tensor
        def _(pe):
            T = nc.tensor
            chunk = [0]

            def next_chunk():
                c = chunk[0]
                pe.wait_ge(slot_full[pre_slot(c)], 16 * (c // EARLY + 1))
                return slot(pre_slot(c))

            def project(g):
                _, _, w, meta = PROJ[g]
                per, q = SLOT // w, w // 4
                first = GROUP_END[g] - chunk[0]
                k0 = 0 if w == 256 or first == 2 else per
                if k0 == 0 and g >= 2:
                    pe.wait_ge(proj_sb, g - 1)
                src = next_chunk()
                for kk in range(per):
                    k = k0 + kk
                    if chunk[0] == 0 and k % 2 == 0:
                        pe.wait_ge(xg_gain, k // 2 + 1)
                    rhs = src[:, kk * w:(kk + 1) * w]
                    if meta:
                        for j in range(4):
                            T.matmul(bank[4][32 * j:32 * j + 32, 0:q], xT[:, k, 0:32], rhs[:, j * q:(j + 1) * q],
                                     start=(k == 0), stop=(k == KT - 1))
                    for t in range(NT):
                        ins = T.matmul(bank[2 * (g % 2) + t][:, 0:w], xT[:, k, tok(t)], rhs, start=(k == 0), stop=(k == KT - 1))
                chunk[0] += 1
                ins.then_inc(chunk_used, 1)

            def transposes(dst, srcs, ids=None):
                w = srcs[0].shape[0]
                for j, src in enumerate(srcs):
                    ins = T.transpose(dst[:, j * w:(j + 1) * w], src, ident if ids is None else ids[j])
                return ins

            def score(t):
                nk = META + P * (t + 1)
                for hd in range(HEADS):
                    i = t * HEADS + hd
                    if i >= 3:
                        pe.wait_ge(score_sb, i - 2)
                    r0 = HD * (hd % 2)
                    T.matmul(bank[5 + (i + 1) % 3][:, 0:nk], qaT[r0:r0 + HD, hd // 2, t * P:(t + 1) * P],
                             kaT[r0:r0 + HD, hd // 4, 0:nk], start=True, stop=True).then_inc(score_ps, 1)

            def transpose_probs(t, q):
                pe.wait_ge(exp_done, t + 1)
                for j in range(4):
                    hd, js = 4 * q + j, slice(j * P, (j + 1) * P)
                    T.transpose(bank[5][0:META, js], prob[t][:, hd, 0:META], ident)
                    ins = T.transpose(bank[6][:, js], prob[t][:, hd, META:META + P], ident)
                    if t:
                        ins = T.transpose(bank[7][:, js], prob[t][:, hd, META + P:KEYS], ident)
                ins.then_inc(pT_ps, 1)

            def values(t, q):
                pe.wait_ge(pT_sb, 2 * t + q + 1)
                if t:
                    pe.wait_ge(pv_sb, 1)
                for j in range(4):
                    hd, vs = 4 * q + j, slice(q * HD, (q + 1) * HD)
                    o = bank[4][:, hd * HD:(hd + 1) * HD]
                    T.matmul(o, pT[0:META, j, 0, :], vam[:, vs], start=True, stop=False)
                    ins = T.matmul(o, pT[:, j, 1, :], va[:, 0, vs], start=False, stop=(t == 0))
                    if t:
                        ins = T.matmul(o, pT[:, j, 2, :], va[:, 1, vs], start=False, stop=True)
                ins.then_inc(pv_ps, 1)

            def products(hd):
                b = bank[(hd + 1) % 2]
                pe.wait_ge(att_sb, hd) if hd else None
                T.matmul(b[:, 0:256], krT[:, hd, tok(0)], qrT[:, hd, :], start=True, stop=True)
                T.matmul(b[:, 256:384], krT[:, hd, tok(1)], qrT[:, hd, P:2 * P], start=True, stop=True).then_inc(att_ps, 1)

            def retain(hd):
                pe.wait_ge(att_sb, hd + 2)
                if hd:
                    pe.wait_ge(ret_ps, hd)
                vs, b, rows = slice(hd * RD, (hd + 1) * RD), attT[hd % 2], slice(32 * hd, 32 * hd + META)
                for t in range(NT):
                    o = ret_bank(t, hd)
                    T.matmul(o, attm[rows, t * P:(t + 1) * P], vrm[rows, :], start=True, stop=False)
                    ins = T.matmul(o, b[:, t * P:(t + 1) * P], vr[:, 0, vs], start=False, stop=(t == 0))
                T.matmul(ret_bank(1, hd), b[:, 256:384], vr[:, 1, vs], start=False, stop=True).then_inc(ret_ps, 1)

            js = [slice(j * P, (j + 1) * P) for j in range(8)]
            pe.wait_ge(ld_tab, 16)
            project(KV)
            project(QA)
            pe.wait_ge(kn_ready, 1)
            for g in range(KV_HEADS):
                ins = transposes(bank[5][:, g * 256:(g + 1) * 256], [kn[:, t, js[g]] for t in range(NT)])
            ins.then_inc(qkT_ps, 1)
            T.transpose(bank[6][:, 0:64], knm, ident[0:64, 0:64]).then_inc(qkT_ps, 1)
            project(QA)
            project(KR)
            pe.wait_ge(qn_ready, 1)
            pe.wait_ge(qkT_sb, 1)
            for t in range(NT):
                transposes(bank[(7, 5)[t]], [nat_q[:, t, js[j]] for j in range(4)]).then_inc(qkT_ps, 1)
            project(KR)
            pe.wait_ge(qkT_sb, 4)
            score(0)
            project(QR)
            score(1)
            project(QR)
            pe.wait_ge(proj_sb, KR + 1)
            pe.wait_ge(score_sb, 2 * HEADS)
            for t in range(NT):
                transposes(bank[5 + t], [nat_k[:, t, js[j]] for j in range(4)]).then_inc(rT_ps, 1)
            T.transpose(bank[7][:, 0:P], krm, ident).then_inc(rT_ps, 1)
            project(VR)
            pe.wait_ge(proj_sb, QR + 1)
            for t in range(NT):
                pe.wait_ge(rT_sb, (3, 1)[t])
                transposes(bank[(7, 5)[t]], [nat_q[:, t, js[j]] for j in range(4)]).then_inc(rT_ps, 1)
            project(VR)
            pe.wait_ge(rT_sb, 5)
            transpose_probs(0, 0)
            project(GR)
            pe.wait_ge(proj_sb, VR + 1)
            values(0, 0)
            transpose_probs(0, 1)
            for j in range(RH):
                ins = T.matmul(bank[0][32 * j:32 * j + 32, 0:SEQ], krT[:, j, 0:32], qrT[:, j, :], start=True, stop=True)
            ins.then_inc(att_ps, 1)
            project(GR)
            values(0, 1)
            transpose_probs(1, 0)
            products(0)
            products(1)
            values(1, 0)
            transpose_probs(1, 1)
            pe.wait_ge(proj_sb, GR + 1)
            retain(0)
            products(2)
            values(1, 1)
            retain(1)
            products(3)
            retain(2)
            retain(3)
            for t in range(NT):
                pe.wait_ge(mix_ready, 3 + t)
                if t == 0:
                    pe.wait_ge(att_sb, RH + 1)
                for q in range(2):
                    transposes(bank[(0, 1, 5, 6)[2 * t + q]], [xr[:, t, js[4 * q + j]] for j in range(4)]).then_inc(mixT_ps, 1)
            w_out = [next_chunk()]
            for c in range(1, 4):
                chunk[0] += 1
                w_out.append(next_chunk())
            for t in range(NT):
                pe.wait_ge(mixT_sb, 2 * t + 2)
                for k in range(KT):
                    for j in range(2):
                        ins = T.matmul(bank[(7, 3, 0, 1)[2 * t + j]][:], xT[:, k, t * P:(t + 1) * P],
                                       w_out[k // 2][:, (k % 2) * D + j * 512:(k % 2) * D + (j + 1) * 512], start=(k == 0), stop=(k == KT - 1))
                    if t == NT - 1 and k % 2:
                        ins.then_inc(chunk_used, 1)
                if t == 0:
                    ins.then_inc(out_ps, 1)
            for t in range(NT):
                pe.wait_ge(xf_ready, t + 1)
                pe.wait_ge(mixT_sb, 4)
                for q in range(2):
                    transposes(bank[(4, 2, 5, 6)[2 * t + q]], [xr[:, t, js[4 * q + j]] for j in range(4)]).then_inc(xfT_ps, 1)
                pe.wait_ge(xfT_sb, 2 * t + 2)
                for k in range(KT):
                    ins = T.matmul(bank[(3, 7)[t]][:, 0:E], xT[:, k, t * P:(t + 1) * P], wr[:, k, :], start=(k == 0), stop=(k == KT - 1))
                ins.then_inc(logit_ps, 1)
            pe.wait_ge(mask_ready, NT)
            pe.wait_ge(ones_set, 1)
            T.matmul(bank[1][:, 0:E], tri, mask[:, 0, :], start=True, stop=True)
            T.matmul(bank[1][:, E:2 * E], ones[:], mask[:, 0, :], start=True, stop=False)
            T.matmul(bank[1][:, E:2 * E], tri, mask[:, 1, :], start=False, stop=True)
            T.matmul(bank[1][:, 2 * E:3 * E], ones[:], mask[:, 0, :], start=True, stop=False)
            T.matmul(bank[1][:, 2 * E:3 * E], ones[:], mask[:, 1, :], start=False, stop=True).then_inc(rank_ps, 1)

            def gather(b):
                for k in range(KT):
                    for i in range(3):
                        for t in range(NT):
                            ins = T.matmul(bank[4][:, k * CAP:(k + 1) * CAP], xs[i][:, t, k * P:(k + 1) * P], sel[b][:, t, :],
                                           start=(i == 0 and t == 0), stop=(i == 2 and t == NT - 1))
                ins.then_inc(xg_ps, 1)

            def spread(t, b):
                for j in range(2):
                    r0 = CAP * j
                    ins = T.matmul(bank[6 + j][:], selT[b][r0:r0 + CAP, t, :], y[r0:r0 + CAP, :], start=True, stop=True)
                ins.then_inc(add_ps, 1)

            pe.wait_ge(sel_ready, 1)
            pe.wait_ge(low_ready, 2 * NT)
            pe.wait_ge(high_sb, 2 * NT)
            gather(0)
            pe.wait_ge(gatew_ready, 1)
            for t in range(NT):
                ins = T.transpose(bank[6][0:E, t * P:(t + 1) * P], gatew[:, t, 0:E], ident)
            ins.then_inc(gT_ps, 1)
            pe.wait_ge(gT_sb, 1)
            pe.wait_ge(ld_bdown, 16)
            for t in range(NT):
                for j in range(2):
                    ins = T.matmul(bank[(2, 3, 6, 7)[2 * t + j]][:], gT[:, t, :], bdown[:, j * 512:(j + 1) * 512], start=True, stop=True)
            ins.then_inc(bd_ps, 1)
            pe.wait_ge(bias_parts, 1)
            pe.wait_ge(bd_sb, 4)
            rounds = pe.value_load(rounds_i[0:1, 0:1], min_val=1, max_val=SEQ // CAP)
            with pe.Fori(0, rounds * GROUPS) as it:
                for u in range(UNROLL):
                    n = it * UNROLL + u
                    pe.wait_ge(pick_ready, n + 1)
                    pe.wait_ge(xg_sb, n + 1)
                    pe.wait_ge(act_sb, n + 1)
                    for f in range(2):
                        for j in range(2):
                            c0 = f * FF + j * 512
                            T.matmul(bank[f][CAP * j:CAP * (j + 1), :], pick[u % 2], bias[:, c0:c0 + 512], start=True, stop=False)
                    for k in range(KT):
                        c = u * EC + k
                        pe.wait_ge(slot_full[moe_slot(c)], it * (16 * TURNS) + 16 * (moe_turn(c) + 1))
                        for f in range(2):
                            for j in range(2):
                                c0 = f * FF + j * 512
                                ins = T.matmul(bank[f][CAP * j:CAP * (j + 1), :], xg[u % 2][:, k, :], slot(moe_slot(c))[:, c0:c0 + 512],
                                               start=False, stop=(k == KT - 1))
                        ins.then_inc(chunk_used, 1)
                    pe.wait_ge(gsel_ready, n + 1)
                    pe.wait_ge(selT_sb, n + 1)
                    for t in range(NT):
                        ins = T.transpose(bank[5][:, t * P:(t + 1) * P], gsel[u % 2][:, t, :], ident)
                    ins.then_inc(selT_ps, 1)
                    pe.wait_ge(y_sb, n + 1)
                    pe.wait_ge(add_sb, n * NT + 1)
                    spread(0, (u + 1) % 2)
                    pe.wait_ge(sel_ready, n + 2)
                    gather((u + 1) % 2)
                    pe.wait_ge(act_sb, n + 2)
                    for jj in range(2):
                        for i in range(2):
                            b = 2 * jj + i
                            ins = T.transpose(bank[3][:, b * P:(b + 1) * P], act_o[:, 256 * jj + i:256 * jj + 256:2], ident)
                    ins.then_inc(actT_ps, 1)
                    pe.wait_ge(add_sb, n * NT + 2)
                    spread(1, (u + 1) % 2)
                    pe.wait_ge(actT_sb, n + 1)
                    for c in range(4):
                        q = u * EC + KT + c
                        pe.wait_ge(slot_full[moe_slot(q)], it * (16 * TURNS) + 16 * (moe_turn(q) + 1))
                        for i in range(2):
                            for j in range(2):
                                lhs = actT[:, 2 * (c % 2) + i, CAP * (c // 2):CAP * (c // 2 + 1)]
                                ins = T.matmul(bank[2][CAP * j:CAP * (j + 1), :], lhs,
                                               slot(moe_slot(q))[:, i * D + j * 512:i * D + (j + 1) * 512],
                                               start=(c == 0 and i == 0), stop=(c == 3 and i == 1))
                        ins.then_inc(chunk_used, 1)
            pe.wait_ge(y_sb, rounds * E + 1)
            pe.wait_ge(add_sb, rounds * (E * NT) + 1)
            spread(0, 1)
            pe.wait_ge(add_sb, rounds * (E * NT) + 2)
            spread(1, 1)


_INS = ["w_in", "w_out", "w_gate_up", "b_gate_up", "w_down", "b_down"]


def kernel(**inputs):
    import concourse.bacc as _bacc
    from concourse.bass_utils import run_bass_kernel_spmd as _run

    nc = _bacc.Bacc("TRN2", target_bir_lowering=False, num_devices=1)
    v = {k: np.asarray(a) for k, a in inputs.items()}
    named = {n: np.ascontiguousarray(v[n]) for n in _INS}
    seq = np.concatenate([v["meta_tokens"], v["x"][0]], 0)
    named["x"] = np.ascontiguousarray(v["x"][0])
    named["xT"] = np.ascontiguousarray(seq.T.reshape(KT, P, KEYS).transpose(1, 0, 2))
    named["x_first"] = np.ascontiguousarray(seq[:32])
    named["small_table"] = small_table(v)
    named["mixer_table"] = mixer_table()
    arrays, aps = {}, {}
    for name, arr in named.items():
        arrays[f"in_{name}"] = arr
        aps[name] = nc.dram_tensor(f"in_{name}", arr.shape, mybir.dt.from_np(arr.dtype), kind="ExternalInput").ap()
    aps["out"] = nc.dram_tensor("out_0", (1, SEQ, D), F32, kind="ExternalOutput").ap()
    build(nc, aps)
    r = _run(nc, [arrays], core_ids=[0])
    return r.results[0]["out_0"]
```

```python
from contextlib import ExitStack

import numpy as np
import concourse.bass as bass
from concourse import mybir

F32 = mybir.dt.float32
BF16 = mybir.dt.bfloat16
I32 = mybir.dt.int32
ALU = mybir.AluOpType
ACT = mybir.ActivationFunctionType
X = mybir.AxisListType.X

P = 128
D = 1024
KT = D // P
SEQ = 256
NT = SEQ // P
META = 16
CHUNK = 64
META_POS = CHUNK - META
KEYS = META + SEQ
HEADS, KV_HEADS, HD = 8, 2, 64
RH, RD = 4, 128
E = 32
CAP = 64
FF = 1024
LIMIT, ALPHA = 7.0, 1.702
EPS = 1e-5
MASKED = -1e32
BIG = 3e38

SLOT = 2048
NSLOT = 17
EARLY = 12
EC = 12
UNROLL = 4
ITER = UNROLL * EC
GROUPS = E // UNROLL

PROJ = [("kv", 512, 256, True), ("qa", 0, 512, False), ("kr", 1280, 512, True),
        ("qr", 768, 512, False), ("vr", 1792, 512, True), ("gr", 2304, 512, False)]
KV, QA, KR, QR, VR, GR = range(6)
IN_CHUNKS = [(g, k, SLOT // p[2]) for g, p in enumerate(PROJ) for k in range(0, KT, SLOT // p[2])]
GROUP_END = [sum(1 for c in IN_CHUNKS if c[0] <= g) for g in range(len(PROJ))]
PRE = len(IN_CHUNKS) + 4
BASE = PRE - EARLY

TAB = {}
for _name, _n in (("ident", P), ("tri", P), ("iota1", P), ("expert", E + 1), ("g_ffn", KT),
                  ("g_out", KT), ("g_q", 1), ("g_k", 1), ("sinks", HEADS), ("slope", HEADS), ("br", E), ("wr", KT * E)):
    TAB[_name] = (sum(n for _, n in TAB.values()), _n)
TAB_W = sum(n for _, n in TAB.values())
MIX_W = NT * KEYS + RH * SEQ + SEQ


def pre_slot(c):
    return c % EARLY


def moe_slot(n):
    i = n % NSLOT
    return i if i == NSLOT - 1 else (BASE + i) % (NSLOT - 1)


def moe_fills(n):
    s = moe_slot(n)
    return sum(1 for c in range(PRE) if pre_slot(c) == s) + n // NSLOT


def moe_turns(n):
    return sum(1 for m in range(ITER) if moe_slot(m) == moe_slot(n))


def moe_last(n):
    return n - NSLOT if n >= NSLOT else max(m for m in range(ITER) if m % NSLOT == n) - ITER


def mixer_table():
    qpos = CHUNK + np.arange(SEQ)
    kpos = np.concatenate([META_POS + np.arange(META), qpos])
    seen = np.zeros((SEQ, KEYS), bool)
    seen[:, :META] = True
    gap = qpos[:, None] // CHUNK - kpos[None, :] // CHUNK
    seen |= (gap >= 0) & (gap <= 1)
    dist = np.where(seen, -np.abs(qpos[:, None] - kpos[None, :]).astype(np.float64), MASKED)
    log_g = np.log1p(-(2.0 ** (-5.0 - np.arange(RH))))
    delta = qpos[None, :] - kpos[:, None]
    decay = np.where(delta >= 0, np.exp(log_g[:, None, None] * np.maximum(delta, 0)), 0.0) * RD ** -0.5
    meta = np.zeros((P, SEQ))
    for j in range(RH):
        meta[32 * j:32 * j + META] = decay[j, :META]
    return np.concatenate([dist.reshape(NT, P, KEYS).transpose(1, 0, 2).reshape(P, -1),
                           decay[:, META:META + P].transpose(1, 0, 2).reshape(P, -1), meta], 1).astype(np.float32)


def small_table(v):
    def cols(a, n):
        return a.reshape(n, P).T

    def rows(a):
        return np.broadcast_to(a.reshape(1, -1), (P, a.size))

    f = np.float32
    t = dict(
        ident=np.eye(P, dtype=f), tri=(np.arange(P)[:, None] < np.arange(P)[None, :]).astype(f),
        iota1=rows((np.arange(P) % CAP + 1).astype(f)),
        expert=((np.arange(P)[:, None] % E) == (np.arange(E + 1)[None, :] % E)).astype(f),
        g_ffn=cols(v["norm_ffn_g"], KT),
        g_out=np.concatenate([cols(v["attn_out_g"], KT // 2), cols(v["ret_norm_g"], KT // 2)], 1),
        g_q=np.tile(v["q_norm_g"][0], 2)[:, None], g_k=np.tile(v["k_norm_g"][0], 2)[:, None],
        sinks=rows(v["attn_sinks"]), slope=rows((2.0 ** (-8.0 * np.arange(1, HEADS + 1) / HEADS)).astype(f)),
        br=rows(v["router_b"]), wr=v["router_w"][0].reshape(KT, P, E).transpose(1, 0, 2).reshape(P, -1))
    return np.ascontiguousarray(np.concatenate([t[k] for k in TAB], 1))


def build(nc, a):
    ctx = ExitStack()
    with ctx:
        def sb(name, shape, dt=F32):
            return ctx.enter_context(nc.sbuf_tensor(name, shape, dt))

        def sem(name):
            return ctx.enter_context(nc.semaphore(name))

        ring = sb("ring", [P, NSLOT * SLOT])
        h = sb("h", [P, NT, D])
        xr = sb("xr", [P, NT, D])
        xT = sb("xT", [P, KT, KEYS])
        table = sb("table", [P, TAB_W])
        ones = sb("ones", [P, P])
        gain = sb("gain", [P, KT])
        bias = sb("bias", [96, 2 * FF], BF16)
        half = sb("half", [P, 16])
        rank = sb("rank", [P, NT, E + 1])
        gatew = sb("gatew", [P, NT, E + 1])
        rounds_i = sb("rounds_i", [1, 1], I32)
        va = sb("va", [P, NT, P])
        vam = sb("vam", [META, P])
        lx = sb("lx", [P, NT, E + 8])
        lrep = sb("lrep", [P, NT, E + 8])
        mask = sb("mask", [P, NT, E])
        eexp = sb("eexp", [P, NT, E])
        small = sb("small", [P, 160])
        area = sb("area", [P, 9216])

        def tab(name):
            c0, n = TAB[name]
            return table[:, c0:c0 + n]

        ident, tri, iota1, expert = tab("ident"), tab("tri"), tab("iota1"), tab("expert")
        g_ffn, g_out, slope, sinks = tab("g_ffn"), tab("g_out"), tab("slope"), tab("sinks")
        wr = tab("wr").rearrange("p (k e) -> p k e", k=KT)

        class Views:
            def __init__(self, tensor, start, end):
                self.t, self.at, self.end = tensor, start, end

            def take(self, parts, *shape, dt=F32):
                n = int(np.prod(shape)) * (2 if dt == BF16 else 4) // 4
                v = self.t[0:parts, self.at:self.at + n]
                self.at += n
                assert self.at <= self.end, (self.at, self.end)
                if dt != F32:
                    v = v.bitcast(dt)
                if len(shape) == 2:
                    v = v.rearrange("p (a b) -> p a b", a=shape[0])
                if len(shape) == 3:
                    v = v.rearrange("p (a b c) -> p a b c", a=shape[0], b=shape[1])
                return v

        m = Views(area, 0, 9216)
        nat_q = m.take(P, NT, 512)
        nat_k = m.take(P, NT, 512)
        krm = m.take(P, RD)
        vrm = m.take(P, RD)
        vr = m.take(P, NT, 512)
        gr = m.take(P, NT, 512)
        qaT = m.take(P, 4, SEQ)
        kaT = m.take(P, KV_HEADS, KEYS)
        qrT = m.take(P, RH, SEQ)
        krT = m.take(P, RH, KEYS)
        assert m.at <= 8192
        ka = vr[:, :, 0:P]
        kn = vr[:, :, P:P + 256]
        kam = vrm[0:64, 0:HD]
        knm = krT.rearrange("p a b -> p (a b)")[0:64, 0:P]
        xm = qrT.rearrange("p a b -> p (a b)")
        osq = nat_k[:, 0, :]
        m = Views(area, 0, 9216)
        xs = [m.take(P, NT, D, dt=BF16) for _ in range(3)]
        sel = [m.take(P, NT, CAP, dt=BF16) for _ in range(2)]
        gsel = [m.take(P, NT, P) for _ in range(2)]
        selT = [m.take(P, NT, P) for _ in range(2)]
        xg = [m.take(P, KT, CAP) for _ in range(2)]
        pick = [m.take(96, CAP, dt=BF16) for _ in range(2)]
        gate = m.take(P, 512)
        sig = m.take(P, 512)
        up = m.take(P, 512)
        act_o = m.take(P, 512)
        actT = m.take(P, 4, P)
        m.at = max(m.at, 8192)
        y = m.take(P, 512)
        m = Views(ring, EARLY * SLOT, (NSLOT - 1) * SLOT)
        mixer_table_sb = ring[:, m.at:m.at + MIX_W]
        dist = m.take(P, NT, KEYS)
        decay = m.take(P, RH, SEQ)
        decaym = m.take(P, SEQ)
        prob = [m.take(P, HEADS, META + P), m.take(P, HEADS, KEYS)]
        at = m.at
        pT = m.take(P, 4, 3, P)
        attT = [m.take(P, 384) for _ in range(2)]
        attm = m.take(P, SEQ)
        m.at = at
        bstage = m.take(96, 2 * FF)
        bhigh = m.take(96, FF, dt=BF16)
        sqk = prob[1].rearrange("p a b -> p (a b)")

        bank = [ctx.enter_context(nc.psum_tensor(f"bank{i}", [P, 512], F32)) for i in range(8)]

        cols = [0]

        def col(n):
            cols[0] += n
            assert cols[0] <= 160
            return small[:, cols[0] - n:cols[0]]

        ssx, ssk, ssq = col(3), col(5), col(16)
        mx, negm, rsum, esink = ([col(HEADS) for _ in range(NT)] for _ in range(4))
        ssa, stats, mv, sso = col(HEADS), col(6), col(2 * NT * RH), col(NT)
        top8, rep8, nmax, den, over = col(8), col(8), col(NT), col(NT), col(5)

        slot_full = [sem(f"slot_full{s}") for s in range(NSLOT)]
        chunk_used = sem("chunk_used")
        ld_x, ld_tab, ld_mix, ld_bias, ld_bdown = (
            sem(f"loaded_{n}") for n in ("x", "table", "mixer_table", "bias", "bdown"))
        ld_gain, ld_xT, slot_half = sem("loaded_gain"), [sem(f"loaded_xT{j}") for j in range(2)], sem("slot0_half")
        stored = sem("stored")
        dv = sem("dve_chain")
        ones_set, half_set = sem("ones_set"), sem("half_set")
        xg_gain = sem("x_times_gain")
        sq_done, var_ready, rstd_ready = sem("squares_summed"), sem("var_ready"), sem("rstd_ready")
        proj_sb = sem("proj_sb")
        bias_parts, bias_low = sem("bias_parts"), sem("bias_low")
        kn_ready, qn_ready = sem("kn_ready"), sem("qn_ready")
        qkT_ps, qkT_sb = sem("qkT_ps"), sem("qkT_sb")
        rT_ps, rT_sb = sem("rT_ps"), sem("rT_sb")
        score_ps, score_sb = sem("score_ps"), sem("score_sb")
        max_ready, exp_done = sem("max_ready"), sem("exp_done")
        pT_ps, pT_sb = sem("pT_ps"), sem("pT_sb")
        pv_ps, pv_sb = sem("pv_ps"), sem("pv_sb")
        att_ps, att_sb = sem("att_ps"), sem("att_sb")
        ret_ps = sem("ret_ps")
        gate_sig = sem("gate_sigmoid")
        mix_ready, mixT_ps, mixT_sb = sem("mix_ready"), sem("mixT_ps"), sem("mixT_sb")
        out_ps, h_ready = sem("out_ps"), sem("h_ready")
        xf_ready, xfT_ps, xfT_sb = sem("xf_ready"), sem("xfT_ps"), sem("xfT_sb")
        high_sb, low_ready = sem("high_part"), sem("rest_ready")
        logit_ps, nmax_ready, e_exp = sem("logit_ps"), sem("nmax_ready"), sem("gate_exp")
        mask_ready, rank_ps, rounds_ready = sem("mask_ready"), sem("rank_ps"), sem("rounds_ready")
        gatew_ready, gT_ps, y_zero, last_ps, last_add = (
            sem("gatew_ready"), sem("gT_ps"), sem("y_zeroed"), sem("last_ps"), sem("last_add"))
        sel_ready, gsel_ready, pick_ready = sem("sel_ready"), sem("gsel_ready"), sem("pick_ready")
        xg_ps, xg_sb = sem("xg_ps"), sem("xg_sb")
        gate_sb, sig_sb, act_sb = sem("gate_sb"), sem("sig_sb"), sem("act_sb")
        selT_ps, selT_sb = sem("selT_ps"), sem("selT_sb")
        actT_ps, actT_sb = sem("actT_ps"), sem("actT_sb")
        y_sb = sem("y_sb")
        add_ps, add_sb = sem("add_ps"), sem("add_sb")

        def ret_bank(t, hd):
            return bank[((3, 5), (2, 6))[t][hd // 2]][:, (hd % 2) * RD:(hd % 2 + 1) * RD]

        block = ctx.enter_context(nc.Block())

        def slot(s):
            return ring[:, s * SLOT:(s + 1) * SLOT]

        def tok(t):
            return slice(META + t * P, META + (t + 1) * P)

        def four(ap):
            return ap.rearrange("p (a b) -> p a b", a=4)

        @block.sync
        def _(sp):
            w_in = a["w_in"][0].rearrange("(k p) n -> p k n", p=P)

            def load_in(c):
                g, k, n = IN_CHUNKS[c]
                _, c0, w, _ = PROJ[g]
                sp.dma_start(slot(pre_slot(c)).rearrange("p (k n) -> p k n", n=w),
                             w_in[:, k:k + n, c0:c0 + w]).then_inc(slot_full[pre_slot(c)], 16)

            sp.dma_start(gain[:], a["g_mix"]).then_inc(ld_gain, 16)
            for j in range(2):
                sp.dma_start(xT[:, 4 * j:4 * j + 4, :], a["xT"][:, 4 * j:4 * j + 4, :]).then_inc(ld_xT[j], 16)
                sp.dma_start(slot(0).rearrange("p (k n) -> p k n", k=KT)[:, 4 * j:4 * j + 4, :],
                             w_in[:, 4 * j:4 * j + 4, 512:768]).then_inc((slot_half, slot_full[0])[j], 16)
            sp.dma_start(table[:], a["small_table"]).then_inc(ld_tab, 16)
            sp.dma_start(h[:], a["x"].rearrange("(t p) d -> p t d", p=P)).then_inc(ld_x, 16)
            for j in range(4):
                sp.dma_start(xm[32 * j:32 * j + 32, :], a["x_first"]).then_inc(ld_x, 16)
            load_in(1)
            load_in(2)
            for j in range(3):
                sp.dma_start(bstage[32 * j:32 * j + 32, :], a["b_gate_up"][0]).then_inc(ld_bias, 16)
            load_in(3)
            sp.dma_start(mixer_table_sb, a["mixer_table"]).then_inc(ld_mix, 16)
            for c in range(4, len(IN_CHUNKS)):
                load_in(c)
            sp.wait_ge(y_zero, 1)
            for j in range(2):
                sp.dma_start(y[CAP * j:CAP * j + E, :], a["b_down"][0][:, j * 512:(j + 1) * 512]).then_inc(ld_bdown, 16)
            w_out = a["w_out"][0].rearrange("(c i p) n -> c p i n", p=P, i=2)
            for j in range(4):
                c = len(IN_CHUNKS) + j
                if c >= EARLY:
                    sp.wait_ge(chunk_used, c - EARLY + 1)
                sp.dma_start(slot(pre_slot(c)).rearrange("p (i n) -> p i n", i=2),
                             w_out[j]).then_inc(slot_full[pre_slot(c)], 16)

            gu = a["w_gate_up"][0].rearrange("e (k p) n -> e k p n", p=P)
            dn = a["w_down"][0].rearrange("e (j p i) n -> e j p (i n)", p=P, i=2)

            def load_group(g, it, first):
                for n in range(ITER):
                    u, c = divmod(n, EC)
                    s = moe_slot(n)
                    if not first or n >= NSLOT:
                        sp.wait_ge(chunk_used, it * ITER + (PRE + moe_last(n) + 1))
                    elif s == EARLY:
                        sp.wait_ge(ret_ps, RH)
                        sp.wait_ge(pv_ps, 2 * NT)
                    elif s < EARLY:
                        sp.wait_ge(chunk_used, (EARLY if s < BASE else 0) + s + 1)
                    src = (gu[bass.ds(g * UNROLL + u, 1), c] if c < KT else dn[bass.ds(g * UNROLL + u, 1), c - KT])
                    sp.dma_start(slot(s), src.rearrange("e p n -> (e p) n")).then_inc(slot_full[s], 16)

            load_group(0, 0, True)
            with sp.Fori(1, GROUPS) as g:
                load_group(g, g, False)
            sp.wait_ge(rounds_ready, 1)
            rounds = sp.value_load(rounds_i[0:1, 0:1], min_val=1, max_val=SEQ // CAP)
            with sp.If(rounds > 1):
                with sp.Fori(1, rounds) as r:
                    with sp.Fori(0, GROUPS) as g:
                        load_group(g, r * GROUPS + g, False)
            for i in range(2 * NT):
                t, cs = i // 2, slice((i % 2) * 512, (i % 2 + 1) * 512)
                sp.wait_ge(last_add, i + 1)
                sp.dma_start(a["out"][0, t * P:(t + 1) * P, cs], h[:, t, cs]).then_inc(stored, 16)
            sp.wait_ge(stored, 16 * 2 * NT)

        @block.gpsimd
        def _(pool):
            G = nc.gpsimd
            G.memset(half[:], -0.5).then_inc(half_set, 1)
            pool.wait_ge(half_set, 1)
            G.memset(ones[:], 1.0).then_inc(ones_set, 1)
            pool.wait_ge(ones_set, 1)
            done = [0]

            def power(*vs):
                for v in vs:
                    if done[0]:
                        pool.wait_ge(rstd_ready, done[0])
                    done[0] += 1
                    pool.wait_ge(var_ready, done[0])
                    G.tensor_tensor(v, v, half[0:v.shape[0], 0:v.shape[1]], ALU.pow).then_inc(rstd_ready, 1)

            power(ssx[:], ssk[:, 0:4], ssk[0:64, 4:5], ssq[:])
            pool.wait_ge(rstd_ready, 4)
            pool.wait_ge(ld_bias, 48)
            rows = slice(32, 64)
            G.tensor_copy(bias[0:32, :], bstage[0:32, :]).then_inc(bias_parts, 1)
            for c in range(2):
                cs = slice(c * FF, (c + 1) * FF)
                pool.wait_ge(bias_parts, 3 * c + 1)
                G.tensor_copy(bhigh[rows, :], bstage[rows, cs]).then_inc(bias_parts, 1)
                pool.wait_ge(bias_parts, 3 * c + 2)
                G.tensor_tensor(bstage[rows, cs], bstage[rows, cs], bhigh[rows, :], ALU.subtract).then_inc(bias_parts, 1)
                pool.wait_ge(bias_parts, 3 * c + 3)
                G.tensor_copy(bias[rows, cs], bstage[rows, cs]).then_inc(bias_parts, 1)
            pool.wait_ge(bias_parts, 7)
            power(*([ssa[:]] * NT), *[mv[:, 2 * RH * t + 1:2 * RH * (t + 1):2] for t in range(NT)],
                  *[sso[:, t:t + 1] for t in range(NT)])

        @block.scalar
        def _(act):
            S = nc.scalar
            act.wait_ge(ld_x, 16 * 5)
            for t in range(NT):
                S.activation(xr[:, t, :], h[:, t, :], ACT.Square, accum_out=ssx[:, t:t + 1])
            S.activation(vr.rearrange("p a b -> p (a b)"), xm, ACT.Square, accum_out=ssx[:, 2:3]).then_inc(sq_done, 1)
            act.wait_ge(rstd_ready, 1)

            def take(g):
                act.wait_ge(chunk_used, GROUP_END[g])
                for t in range(NT):
                    src = bank[2 * (g % 2) + t]
                    if g == KV:
                        S.activation(ka[:, t, :], src[:, 0:P], ACT.Copy, scale=ssx[:, t:t + 1])
                        last = S.activation(va[:, t, :], src[:, P:2 * P], ACT.Copy, scale=ssx[:, t:t + 1])
                    else:
                        dst = {QA: nat_q, QR: nat_q, KR: nat_k, VR: vr, GR: gr}[g]
                        last = S.activation(dst[:, t, :], src[:], ACT.Copy, scale=ssx[:, t:t + 1])
                if g == KV:
                    S.activation(kam, bank[4][0:64, 0:HD], ACT.Copy, scale=ssx[0:64, 2:3])
                    for j in range(KV_HEADS):
                        r0 = 64 + 32 * j
                        last = S.activation(vam[:, j * HD:(j + 1) * HD], bank[4][r0:r0 + META, 0:HD], ACT.Copy,
                                            scale=ssx[0:META, 2:3])
                elif g in (KR, VR):
                    last = S.activation({KR: krm, VR: vrm}[g], bank[4][:, 0:RD], ACT.Copy, scale=ssx[:, 2:3])
                last.then_inc(proj_sb, 1)

            def softmax_exp(t):
                act.wait_ge(max_ready, t + 1)
                for hd in range(HEADS):
                    S.activation(prob[t][:, hd, :], prob[t][:, hd, :], ACT.Exp, bias=negm[t][:, hd:hd + 1],
                                 accum_out=rsum[t][:, hd:hd + 1])
                S.activation(esink[t], esink[t], ACT.Exp).then_inc(exp_done, 1)

            def take_rT(i):
                act.wait_ge(rT_ps, i + 1)
                src = bank[(5, 6, 7, 7, 5)[i]]
                if i == 2:
                    S.copy(krT[:, :, 0:META], four(src[:, 0:P])[:, :, 0:META]).then_inc(rT_sb, 1)
                elif i < 2:
                    S.copy(krT[:, :, tok(i)], four(src[:])).then_inc(rT_sb, 1)
                else:
                    S.copy(qrT[:, :, (i - 3) * P:(i - 2) * P], four(src[:])).then_inc(rT_sb, 1)

            def take_pT(t, q):
                act.wait_ge(pT_ps, 2 * t + q + 1)
                S.copy(pT[0:META, :, 0, :], four(bank[5][0:META, :]))
                last = S.copy(pT[:, :, 1, :], four(bank[6][:]))
                if t:
                    last = S.copy(pT[:, :, 2, :], four(bank[7][:]))
                last.then_inc(pT_sb, 1)

            take(KV)
            take(QA)
            act.wait_ge(qkT_ps, 2)
            take(KR)
            softmax_exp(0)
            softmax_exp(1)
            for i in range(3):
                take_rT(i)
            act.wait_ge(qkT_ps, 4)
            take(QR)
            act.wait_ge(bias_parts, 7)
            act.wait_ge(bias_low, 2)
            take_rT(3)
            take_rT(4)
            take_pT(0, 0)
            take(VR)
            act.wait_ge(pv_ps, 1)
            take_pT(0, 1)
            take(GR)
            act.wait_ge(proj_sb, GR + 1)
            for t in range(NT):
                S.activation(xr[:, t, 512:1024], gr[:, t, :], ACT.Sigmoid).then_inc(gate_sig, 1)
            act.wait_ge(pv_ps, 2)
            take_pT(1, 0)
            act.wait_ge(pv_ps, 3)
            take_pT(1, 1)
            def squares(t):
                act.wait_ge(h_ready, t + 1)
                S.activation(xr[:, t, :], h[:, t, :], ACT.Square, accum_out=sso[:, t:t + 1]).then_inc(sq_done, 1)

            def high_part(t):
                act.wait_ge(xf_ready, t + 1)
                S.copy(xs[0][:, t, :], xr[:, t, :]).then_inc(high_sb, 1)

            def middle_part(t):
                act.wait_ge(low_ready, 2 * t + 1)
                S.copy(xs[1][:, t, :], xr[:, t, :]).then_inc(high_sb, 1)

            squares(0)
            high_part(0)
            squares(1)
            middle_part(0)
            high_part(1)
            middle_part(1)
            for t in range(NT):
                act.wait_ge(nmax_ready, t + 1)
                S.activation(eexp[:, t, :], lx[:, t, 0:E], ACT.Exp, bias=nmax[:, t:t + 1]).then_inc(e_exp, 1)
            act.wait_ge(gT_ps, 1)
            S.copy(selT[1], bank[5][:, 0:NT * P].rearrange("p (a b) -> p a b", a=NT)).then_inc(selT_sb, 1)

            act.wait_ge(rounds_ready, 1)
            rounds = act.value_load(rounds_i[0:1, 0:1], min_val=1, max_val=SEQ // CAP)
            with act.Fori(0, rounds * GROUPS) as it:
                for u in range(UNROLL):
                    n = it * UNROLL + u
                    act.wait_ge(selT_ps, n + 1)
                    S.copy(selT[u % 2], bank[5][:, 0:NT * P].rearrange("p (a b) -> p a b", a=NT)).then_inc(selT_sb, 1)
                    act.wait_ge(gate_sb, n + 1)
                    S.activation(sig, gate, ACT.Sigmoid, scale=ALPHA).then_inc(sig_sb, 1)
                    act.wait_ge(actT_ps, n + 1)
                    S.copy(actT, four(bank[3][:])).then_inc(actT_sb, 1)
                    act.wait_ge(chunk_used, it * ITER + (PRE + (u + 1) * EC))
                    S.copy(y, bank[2][:]).then_inc(y_sb, 1)

        @block.vector
        def _(dve):
            cnt = [0]
            var = [0]
            V = nc.vector

            def link(ins):
                cnt[0] += 1
                ins.then_inc(dv, 1)
                dve.wait_ge(dv, cnt[0])

            def variance(v, n):
                V.tensor_scalar(v, v, 1.0 / n, EPS, ALU.mult, ALU.add).then_inc(var_ready, 1)
                var[0] += 1

            def rstd_wait(behind=0):
                dve.wait_ge(rstd_ready, var[0] - behind)

            def spread_cols(ap, n, w):
                return ap.unsqueeze(2).broadcast_to([ap.shape[0], n, w])

            V.memset(y, 0.0).then_inc(y_zero, 1)
            dve.wait_ge(ld_gain, 16)
            for k in range(0, KT, 2):
                dve.wait_ge(ld_xT[k // 4], 16)
                V.tensor_tensor(xT[:, k:k + 2, :], xT[:, k:k + 2, :], spread_cols(gain[:, k:k + 2], 2, KEYS), ALU.mult).then_inc(xg_gain, 1)
            dve.wait_ge(sq_done, 1)
            variance(ssx[:], D)
            dve.wait_ge(ld_tab, 16)
            dve.wait_ge(proj_sb, 1)
            sk = sqk[:, 0:256]
            link(V.tensor_tensor(sk.rearrange("p (a b) -> p a b", a=NT), ka, ka, ALU.mult))
            link(V.tensor_reduce(ssk[:, 0:4], four(sk), X, ALU.add))
            variance(ssk[:, 0:4], HD)
            link(V.tensor_tensor(sqk[0:64, 256:320], kam, kam, ALU.mult))
            link(V.tensor_reduce(ssk[0:64, 4:5], sqk[0:64, 256:320], X, ALU.add))
            variance(ssk[0:64, 4:5], HD)
            rstd_wait(1)
            for t in range(NT):
                for g in range(KV_HEADS):
                    link(V.tensor_scalar(kn[:, t, g * P:(g + 1) * P].rearrange("p (a b) -> p a b", a=2),
                                         ka[:, t, g * HD:(g + 1) * HD].unsqueeze(1).broadcast_to([P, 2, HD]),
                                         ssk[:, 2 * t + g:2 * t + g + 1], None, ALU.mult))
            rstd_wait()
            V.tensor_scalar(knm.rearrange("p (a b) -> p a b", a=2), kam.unsqueeze(1).broadcast_to([64, 2, HD]),
                            ssk[0:64, 4:5], None, ALU.mult).then_inc(kn_ready, 1)
            dve.wait_ge(qkT_ps, 1)
            V.tensor_scalar(kaT[:, :, META:KEYS], bank[5][:].rearrange("p (a b) -> p a b", a=2),
                            tab("g_k"), None, ALU.mult).then_inc(qkT_sb, 1)
            dve.wait_ge(qkT_ps, 2)
            V.tensor_scalar(kaT[:, :, 0:META], bank[6][:, 0:64].rearrange("p (a b) -> p a b", a=2)[:, :, 0:META],
                            tab("g_k"), None, ALU.mult).then_inc(qkT_sb, 1)
            dve.wait_ge(proj_sb, 2)
            sq = sqk[:, 0:1024]
            link(V.tensor_tensor(sq.rearrange("p (a b) -> p a b", a=NT), nat_q, nat_q, ALU.mult))
            link(V.tensor_reduce(ssq[:], sq.rearrange("p (a b) -> p a b", a=16), X, ALU.add))
            variance(ssq[:], HD)
            rstd_wait()
            nq = nat_q.rearrange("p t (a b) -> p (t a) b", b=HD)
            V.tensor_tensor(nq, nq, spread_cols(ssq, 16, HD), ALU.mult).then_inc(qn_ready, 1)
            for t in range(NT):
                dve.wait_ge(qkT_ps, 3 + t)
                V.tensor_scalar(qaT[:, :, t * P:(t + 1) * P], four(bank[(7, 5)[t]][:]),
                                tab("g_q"), HD ** -0.5, ALU.mult, ALU.mult).then_inc(qkT_sb, 1)
            dve.wait_ge(ld_bias, 48)
            rows = slice(64, 96)
            for c in range(2):
                cs = slice(c * FF, (c + 1) * FF)
                for _ in range(2):
                    link(V.tensor_copy(bhigh[rows, :], bstage[rows, cs]))
                    link(V.tensor_tensor(bstage[rows, cs], bstage[rows, cs], bhigh[rows, :], ALU.subtract))
                V.tensor_copy(bias[rows, cs], bstage[rows, cs]).then_inc(bias_low, 1)
            dve.wait_ge(bias_low, 2)
            dve.wait_ge(ld_mix, 16)
            for t in range(NT):
                nk = META + P * (t + 1)
                for hd in range(HEADS):
                    i = t * HEADS + hd
                    dve.wait_ge(score_ps, i + 1)
                    V.scalar_tensor_tensor(prob[t][:, hd, :], dist[:, t, 0:nk], slope[:, hd:hd + 1], bank[5 + (i + 1) % 3][:, 0:nk],
                                           ALU.mult, ALU.add).then_inc(score_sb, 1)
                dve.wait_ge(score_sb, HEADS * (t + 1))
                link(V.tensor_reduce(mx[t], prob[t], X, ALU.max))
                link(V.tensor_tensor(mx[t], mx[t], sinks, ALU.max))
                link(V.tensor_tensor(esink[t], sinks, mx[t], ALU.subtract))
                V.tensor_scalar(negm[t], mx[t], -1.0, None, ALU.mult).then_inc(max_ready, 1)
            for t in range(NT):
                dve.wait_ge(exp_done, t + 1)
                link(V.tensor_tensor(rsum[t], rsum[t], esink[t], ALU.add))
                link(V.reciprocal(rsum[t], rsum[t]))

            def attention_norm(t):
                dve.wait_ge(pv_ps, 2 * t + 2)
                o = xr[:, t, 0:512].rearrange("p (a b) -> p a b", a=HEADS)
                sqv = osq.rearrange("p (a b) -> p a b", a=HEADS)
                V.tensor_tensor(o, bank[4][:].rearrange("p (a b) -> p a b", a=HEADS), spread_cols(rsum[t], HEADS, HD),
                                ALU.mult).then_inc(pv_sb, 1)
                dve.wait_ge(pv_sb, t + 1)
                link(V.tensor_tensor(sqv, o, o, ALU.mult))
                link(V.tensor_reduce(ssa[:], sqv, X, ALU.add))
                variance(ssa[:], HD)
                rstd_wait()
                V.tensor_tensor(o, o, spread_cols(ssa, HEADS, HD), ALU.mult).then_inc(mix_ready, 1)

            def times_decay(hd):
                dve.wait_ge(att_ps, 2 + hd)
                if hd >= 2:
                    dve.wait_ge(ret_ps, hd - 1)
                src, dst = bank[(hd + 1) % 2], attT[hd % 2]
                V.tensor_tensor(dst[:, 0:256], src[:, 0:256], decay[:, hd, :], ALU.mult)
                V.tensor_tensor(dst[:, 256:384], src[:, 256:384], decay[:, hd, 0:P], ALU.mult).then_inc(att_sb, 1)

            dve.wait_ge(att_ps, 1)
            V.tensor_tensor(attm, bank[0][:, 0:SEQ], decaym, ALU.mult).then_inc(att_sb, 1)
            attention_norm(0)
            times_decay(0)
            times_decay(1)
            dve.wait_ge(gate_sig, NT)
            link(V.tensor_tensor(gr, gr, xr[:, :, 512:1024], ALU.mult))

            def group_stats(hd):
                dve.wait_ge(ret_ps, 2 * (hd // 2) + 2)
                for t in range(NT):
                    o = 2 * (RH * t + hd)
                    link(V.bn_stats(stats[:], ret_bank(t, hd)))
                    link(V.bn_aggr(mv[:, o:o + 2], stats[:]))

            def take_mixT(t, q):
                dve.wait_ge(mixT_ps, 2 * q + t + 1)
                V.tensor_tensor(xT[:, 4 * q:4 * q + 4, t * P:(t + 1) * P], four(bank[(7, 4, 3, 2)[2 * q + t]][:]),
                                spread_cols(g_out[:, 4 * q:4 * q + 4], 4, P), ALU.mult).then_inc(mixT_sb, 1)

            times_decay(2)
            times_decay(3)
            attention_norm(1)
            take_mixT(0, 0)
            take_mixT(1, 0)
            for hd in range(RH):
                group_stats(hd)
            for t in range(NT):
                V.tensor_scalar(mv[:, 2 * RH * t + 1:2 * RH * (t + 1):2], mv[:, 2 * RH * t + 1:2 * RH * (t + 1):2],
                                1.0, EPS, ALU.mult, ALU.add).then_inc(var_ready, 1)
                var[0] += 1
            for t in range(NT):
                for hd in range(RH):
                    rs = slice(hd * RD, (hd + 1) * RD)
                    o = 2 * (RH * t + hd)
                    link(V.scalar_tensor_tensor(xr[:, t, 512 + hd * RD:512 + (hd + 1) * RD], ret_bank(t, hd), mv[:, o:o + 1],
                                                gr[:, t, rs], ALU.subtract, ALU.mult))
                rstd_wait(1 - t)
                o = xr[:, t, 512:1024].rearrange("p (a b) -> p a b", a=RH)
                V.tensor_tensor(o, o, spread_cols(mv[:, 2 * RH * t + 1:2 * RH * (t + 1):2], RH, RD), ALU.mult).then_inc(mix_ready, 1)
            take_mixT(0, 1)
            take_mixT(1, 1)
            link(V.memset(lx[:, :, E:E + 8], -BIG))
            link(V.memset(rep8[:], -BIG))
            link(V.memset(gsel[1], 0.0))
            def add_mix(t, j):
                return V.tensor_tensor(h[:, t, j * 512:(j + 1) * 512], h[:, t, j * 512:(j + 1) * 512],
                                       bank[(0, 1, 7, 4)[2 * t + j]][:], ALU.add)

            def normalise_h(t):
                dve.wait_ge(sq_done, 2 + t)
                variance(sso[:, t:t + 1], D)
                rstd_wait()
                V.tensor_scalar(xr[:, t, :], h[:, t, :], sso[:, t:t + 1], None, ALU.mult).then_inc(xf_ready, 1)

            def take_hT(t):
                for q in range(2):
                    dve.wait_ge(xfT_ps, 2 * t + q + 1)
                    V.tensor_tensor(xT[:, 4 * q:4 * q + 4, t * P:(t + 1) * P], four(bank[(5, 6, 3, 2)[2 * t + q]][:]),
                                    spread_cols(g_ffn[:, 4 * q:4 * q + 4], 4, P), ALU.mult).then_inc(xfT_sb, 1)

            def rest(t):
                dve.wait_ge(high_sb, 2 * t + 1)
                V.tensor_tensor(xr[:, t, :], xr[:, t, :], xs[0][:, t, :], ALU.subtract).then_inc(low_ready, 1)

            def low_part(t):
                dve.wait_ge(high_sb, 2 * t + 2)
                V.tensor_tensor(xs[2][:, t, :], xr[:, t, :], xs[1][:, t, :], ALU.subtract).then_inc(low_ready, 1)

            def choose(t):
                dve.wait_ge(logit_ps, t + 1)
                link(V.tensor_tensor(lx[:, t, 0:E], bank[(0, 7)[t]][:, 0:E], tab("br"), ALU.add))
                link(V.max(top8[:], lx[:, t, 0:E]))
                link(V.tensor_copy(rep8[:, 0:4], top8[:, 0:4]))
                V.tensor_scalar(nmax[:, t:t + 1], top8[:, 0:1], -1.0, None, ALU.mult).then_inc(nmax_ready, 1)
                link(V.match_replace(lrep[:, t, :], rep8[:], lx[:, t, :], BIG))
                V.tensor_scalar(mask[:, t, :], lrep[:, t, 0:E], BIG, None, ALU.is_equal).then_inc(mask_ready, 1)

            dve.wait_ge(out_ps, 1)
            link(add_mix(0, 0))
            add_mix(0, 1).then_inc(h_ready, 1)
            normalise_h(0)
            dve.wait_ge(out_ps, 2)
            link(add_mix(1, 0))
            take_hT(0)
            dve.wait_ge(chunk_used, PRE)
            add_mix(1, 1).then_inc(h_ready, 1)
            rest(0)
            normalise_h(1)
            low_part(0)
            take_hT(1)
            choose(0)
            rest(1)
            choose(1)
            low_part(1)
            dve.wait_ge(mask_ready, NT)
            dve.wait_ge(rank_ps, 1)
            for t in range(NT):
                link(V.scalar_tensor_tensor(rank[:, t, 0:E], bank[1][:, t * E:(t + 1) * E], 1.0, mask[:, t, :], ALU.add, ALU.mult))
            link(V.tensor_scalar(rank[:, :, E:E + 1], rank[:, :, 0:1], float(CAP), None, ALU.subtract))

            def make_sel(e, b):
                for t in range(NT):
                    ins = V.tensor_scalar(sel[b][:, t, :], iota1[:, 0:CAP], rank[:, t, bass.ds(e, 1)], None, ALU.is_equal)
                ins.then_inc(sel_ready, 1)
                V.tensor_copy(pick[b], expert[0:96, bass.ds(e, 1)].broadcast_to([96, CAP])).then_inc(pick_ready, 1)

            def make_gsel(e, b):
                for t in range(NT):
                    ins = V.tensor_scalar(gsel[b][:, t, :], iota1, rank[:, t, bass.ds(e, 1)], gatew[:, t, bass.ds(e, 1)],
                                          ALU.is_equal, ALU.mult)
                ins.then_inc(gsel_ready, 1)

            def take_xg(b):
                V.tensor_tensor(xg[b], bank[4][:].rearrange("p (a b) -> p a b", a=KT), spread_cols(g_ffn, KT, CAP),
                                ALU.mult).then_inc(xg_sb, 1)

            make_sel(0, 0)
            link(V.tensor_reduce(over[:, 3:4], bank[1][:, 2 * E:3 * E], X, ALU.max))
            for j in range(3):
                link(V.tensor_scalar(over[:, j:j + 1], over[:, 3:4], CAP * (j + 1) + 0.5, None, ALU.is_gt))
            link(V.tensor_reduce(over[:, 4:5], over[:, 0:3], X, ALU.add))
            V.tensor_scalar(rounds_i[:], over[0:1, 4:5], 1.0, None, ALU.add).then_inc(rounds_ready, 1)
            dve.wait_ge(e_exp, NT)
            link(V.tensor_tensor(gatew[:, :, 0:E], eexp[:], mask[:], ALU.mult))
            link(V.tensor_reduce(den[:], gatew[:, :, 0:E], X, ALU.add))
            link(V.reciprocal(den[:], den[:]))
            link(V.tensor_tensor(gatew[:, :, 0:E], gatew[:, :, 0:E], spread_cols(den, NT, E), ALU.mult))
            link(V.tensor_copy(gatew[:, :, E:E + 1], gatew[:, :, 0:1]))
            for c in (0, CAP):
                V.tensor_copy(gsel[1][:, :, c:c + E], gatew[:, :, 0:E]).then_inc(gatew_ready, 1)
            dve.wait_ge(xg_ps, 1)
            take_xg(0)
            V.memset(act_o[:, 0:1], 0.0).then_inc(act_sb, 1)
            V.memset(over[:, 0:1], 0.0).then_inc(add_sb, 1)
            V.memset(over[:, 1:2], 0.0).then_inc(y_sb, 1)
            dve.wait_ge(act_sb, 1)
            dve.wait_ge(add_sb, 1)

            rounds = dve.value_load(rounds_i[0:1, 0:1], min_val=1, max_val=SEQ // CAP)
            CH = 4
            with dve.Fori(0, rounds) as r:
                with dve.Fori(0, GROUPS) as g:
                    for u in range(UNROLL):
                        n = (r * GROUPS + g) * UNROLL + u
                        e = g * UNROLL + u
                        loc = [0]

                        def step(ins):
                            loc[0] += 1
                            ins.then_inc(dv, 1)
                            dve.wait_ge(dv, n * CH + r + (cnt[0] + loc[0]))

                        make_sel(e + 1, (u + 1) % 2)
                        make_gsel(e, u % 2)
                        for t in range(NT):
                            dve.wait_ge(add_ps, (n * NT) + (t + 1))
                            for j in range(2):
                                o = h[:, t, j * 512:(j + 1) * 512]
                                ins = V.tensor_tensor(o, o, bank[6 + j][:], ALU.add)
                                if j == 0:
                                    step(ins)
                            ins.then_inc(add_sb, 1)
                        dve.wait_ge(chunk_used, (r * GROUPS + g) * ITER + (PRE + u * EC + KT))
                        V.tensor_scalar(gate, bank[0][:], LIMIT, None, ALU.min).then_inc(gate_sb, 1)
                        step(V.tensor_scalar(up, bank[1][:], LIMIT, -LIMIT, ALU.min, ALU.max))
                        dve.wait_ge(gate_sb, n + 1)
                        step(V.scalar_tensor_tensor(up, up, 1.0, gate, ALU.add, ALU.mult))
                        dve.wait_ge(sig_sb, n + 1)
                        V.tensor_tensor(act_o, up, sig, ALU.mult).then_inc(act_sb, 1)
                        dve.wait_ge(add_sb, n * NT + (NT + 1))
                        dve.wait_ge(xg_ps, n + 2)
                        take_xg((u + 1) % 2)
                        assert loc[0] == CH
                V.tensor_scalar(rank[:], rank[:], float(CAP), None, ALU.subtract).then_inc(dv, 1)
                dve.wait_ge(dv, r * (E * CH + 1) + (E * CH + 1 + cnt[0]))
            for i in range(2 * NT):
                t, j = divmod(i, 2)
                dve.wait_ge(last_ps, i + 1)
                if i:
                    dve.wait_ge(last_add, i)
                o = h[:, t, j * 512:(j + 1) * 512]
                V.tensor_tensor(o, o, bank[(6, 0)[t] + j][:], ALU.add).then_inc(last_add, 1)

        @block.tensor
        def _(pe):
            T = nc.tensor
            chunk = [0]

            def next_chunk():
                c = chunk[0]
                pe.wait_ge(slot_full[pre_slot(c)], 16 * (c // EARLY + 1))
                return slot(pre_slot(c))

            def project(g):
                _, _, w, meta = PROJ[g]
                per, q = SLOT // w, w // 4
                first = GROUP_END[g] - chunk[0]
                k0 = 0 if w == 256 or first == 2 else per
                if k0 == 0 and g >= 2:
                    pe.wait_ge(proj_sb, g - 1)
                if chunk[0] == 0:
                    src = slot(0)
                    pe.wait_ge(slot_half, 16)
                else:
                    src = next_chunk()
                for kk in range(per):
                    k = k0 + kk
                    if chunk[0] == 0 and k == 4:
                        next_chunk()
                    if chunk[0] == 0 and k % 2 == 0:
                        pe.wait_ge(xg_gain, k // 2 + 1)
                    rhs = src[:, kk * w:(kk + 1) * w]
                    if meta:
                        for j in range(4):
                            T.matmul(bank[4][32 * j:32 * j + 32, 0:q], xT[:, k, 0:32], rhs[:, j * q:(j + 1) * q],
                                     start=(k == 0), stop=(k == KT - 1))
                    for t in range(NT):
                        ins = T.matmul(bank[2 * (g % 2) + t][:, 0:w], xT[:, k, tok(t)], rhs, start=(k == 0), stop=(k == KT - 1))
                chunk[0] += 1
                ins.then_inc(chunk_used, 1)

            def transposes(dst, srcs, ids=None):
                w = srcs[0].shape[0]
                for j, src in enumerate(srcs):
                    ins = T.transpose(dst[:, j * w:(j + 1) * w], src, ident if ids is None else ids[j])
                return ins

            def score(t):
                nk = META + P * (t + 1)
                for hd in range(HEADS):
                    i = t * HEADS + hd
                    if i >= 3:
                        pe.wait_ge(score_sb, i - 2)
                    r0 = HD * (hd % 2)
                    T.matmul(bank[5 + (i + 1) % 3][:, 0:nk], qaT[r0:r0 + HD, hd // 2, t * P:(t + 1) * P],
                             kaT[r0:r0 + HD, hd // 4, 0:nk], start=True, stop=True).then_inc(score_ps, 1)

            def transpose_probs(t, q):
                pe.wait_ge(exp_done, t + 1)
                for j in range(4):
                    hd, js = 4 * q + j, slice(j * P, (j + 1) * P)
                    T.transpose(bank[5][0:META, js], prob[t][:, hd, 0:META], ident)
                    ins = T.transpose(bank[6][:, js], prob[t][:, hd, META:META + P], ident)
                    if t:
                        ins = T.transpose(bank[7][:, js], prob[t][:, hd, META + P:KEYS], ident)
                ins.then_inc(pT_ps, 1)

            def values(t, q):
                pe.wait_ge(pT_sb, 2 * t + q + 1)
                if t:
                    pe.wait_ge(pv_sb, 1)
                for j in range(4):
                    hd, vs = 4 * q + j, slice(q * HD, (q + 1) * HD)
                    o = bank[4][:, hd * HD:(hd + 1) * HD]
                    T.matmul(o, pT[0:META, j, 0, :], vam[:, vs], start=True, stop=False)
                    ins = T.matmul(o, pT[:, j, 1, :], va[:, 0, vs], start=False, stop=(t == 0))
                    if t:
                        ins = T.matmul(o, pT[:, j, 2, :], va[:, 1, vs], start=False, stop=True)
                ins.then_inc(pv_ps, 1)

            def products(hd):
                b = bank[(hd + 1) % 2]
                pe.wait_ge(att_sb, hd) if hd else None
                T.matmul(b[:, 0:256], krT[:, hd, tok(0)], qrT[:, hd, :], start=True, stop=True)
                T.matmul(b[:, 256:384], krT[:, hd, tok(1)], qrT[:, hd, P:2 * P], start=True, stop=True).then_inc(att_ps, 1)

            def retain(hd):
                pe.wait_ge(att_sb, hd + 2)
                if hd:
                    pe.wait_ge(ret_ps, hd)
                vs, b, rows = slice(hd * RD, (hd + 1) * RD), attT[hd % 2], slice(32 * hd, 32 * hd + META)
                for t in range(NT):
                    o = ret_bank(t, hd)
                    T.matmul(o, attm[rows, t * P:(t + 1) * P], vrm[rows, :], start=True, stop=False)
                    ins = T.matmul(o, b[:, t * P:(t + 1) * P], vr[:, 0, vs], start=False, stop=(t == 0))
                T.matmul(ret_bank(1, hd), b[:, 256:384], vr[:, 1, vs], start=False, stop=True).then_inc(ret_ps, 1)

            js = [slice(j * P, (j + 1) * P) for j in range(8)]
            project(KV)
            project(QA)
            pe.wait_ge(ld_tab, 16)
            pe.wait_ge(kn_ready, 1)
            for g in range(KV_HEADS):
                ins = transposes(bank[5][:, g * 256:(g + 1) * 256], [kn[:, t, js[g]] for t in range(NT)])
            ins.then_inc(qkT_ps, 1)
            T.transpose(bank[6][:, 0:64], knm, ident[0:64, 0:64]).then_inc(qkT_ps, 1)
            project(QA)
            project(KR)
            pe.wait_ge(qn_ready, 1)
            pe.wait_ge(qkT_sb, 1)
            for t in range(NT):
                transposes(bank[(7, 5)[t]], [nat_q[:, t, js[j]] for j in range(4)]).then_inc(qkT_ps, 1)
            project(KR)
            pe.wait_ge(qkT_sb, 4)
            score(0)
            project(QR)
            score(1)
            project(QR)
            pe.wait_ge(proj_sb, KR + 1)
            pe.wait_ge(score_sb, 2 * HEADS)
            for t in range(NT):
                transposes(bank[5 + t], [nat_k[:, t, js[j]] for j in range(4)]).then_inc(rT_ps, 1)
            T.transpose(bank[7][:, 0:P], krm, ident).then_inc(rT_ps, 1)
            project(VR)
            pe.wait_ge(proj_sb, QR + 1)
            for t in range(NT):
                pe.wait_ge(rT_sb, (3, 1)[t])
                transposes(bank[(7, 5)[t]], [nat_q[:, t, js[j]] for j in range(4)]).then_inc(rT_ps, 1)
            project(VR)
            pe.wait_ge(rT_sb, 5)
            transpose_probs(0, 0)
            project(GR)
            pe.wait_ge(proj_sb, VR + 1)
            values(0, 0)
            transpose_probs(0, 1)
            for j in range(RH):
                ins = T.matmul(bank[0][32 * j:32 * j + 32, 0:SEQ], krT[:, j, 0:32], qrT[:, j, :], start=True, stop=True)
            ins.then_inc(att_ps, 1)
            project(GR)
            values(0, 1)
            transpose_probs(1, 0)
            products(0)
            products(1)
            values(1, 0)
            transpose_probs(1, 1)
            pe.wait_ge(proj_sb, GR + 1)
            retain(0)
            products(2)
            values(1, 1)
            retain(1)
            products(3)
            retain(2)
            retain(3)
            w_out = []

            def project_out(t, k, j):
                return T.matmul(bank[(0, 1, 7, 4)[2 * t + j]][:], xT[:, k, t * P:(t + 1) * P],
                                w_out[k // 2][:, (k % 2) * D + j * 512:(k % 2) * D + (j + 1) * 512], start=(k == 0), stop=(k == KT - 1))

            def transpose_h(t):
                pe.wait_ge(xf_ready, t + 1)
                for q in range(2):
                    transposes(bank[(5, 6, 3, 2)[2 * t + q]], [xr[:, t, js[4 * q + j]] for j in range(4)]).then_inc(xfT_ps, 1)

            def router_logits(t):
                for k in range(KT):
                    if k % 4 == 0:
                        pe.wait_ge(xfT_sb, 2 * t + k // 4 + 1)
                    ins = T.matmul(bank[(0, 7)[t]][:, 0:E], xT[:, k, t * P:(t + 1) * P], wr[:, k, :], start=(k == 0), stop=(k == KT - 1))
                ins.then_inc(logit_ps, 1)

            for q in range(2):
                for t in range(NT):
                    if q == 0:
                        pe.wait_ge(mix_ready, t + 1)
                        pe.wait_ge(pT_sb, 2 * NT)
                    else:
                        pe.wait_ge(mix_ready, 3 + t)
                    transposes(bank[(7, 4, 3, 2)[2 * q + t]], [xr[:, t, js[4 * q + j]] for j in range(4)]).then_inc(mixT_ps, 1)
                for _ in range(2):
                    w_out.append(next_chunk())
                    chunk[0] += 1
                if q == 0:
                    pe.wait_ge(att_sb, RH + 1)
                for t in range(NT - q):
                    pe.wait_ge(mixT_sb, 2 * q + t + 1)
                    for k in range(4 * q, 4 * q + 4):
                        for j in range(2):
                            ins = project_out(t, k, j)
                        if t == NT - 1 and k % 2:
                            ins.then_inc(chunk_used, 1)
            ins.then_inc(out_ps, 1)
            pe.wait_ge(mixT_sb, 4)
            for k in range(4, 8):
                ins = project_out(1, k, 0)
            ins.then_inc(out_ps, 1)
            for k in range(4, 8):
                ins = project_out(1, k, 1)
                if k == 5:
                    ins.then_inc(chunk_used, 1)
                    transpose_h(0)
            ins.then_inc(chunk_used, 1)
            router_logits(0)
            transpose_h(1)
            router_logits(1)
            pe.wait_ge(mask_ready, 1)
            pe.wait_ge(ones_set, 1)
            T.matmul(bank[1][:, 0:E], tri, mask[:, 0, :], start=True, stop=True)
            T.matmul(bank[1][:, E:3 * E].rearrange("p (a b) -> p a b", a=2), ones[:],
                     mask[:, 0, :].unsqueeze(1).broadcast_to([P, 2, E]), start=True, stop=False)
            pe.wait_ge(mask_ready, 2)
            T.matmul(bank[1][:, E:2 * E], tri, mask[:, 1, :], start=False, stop=False)
            T.matmul(bank[1][:, 2 * E:3 * E], ones[:], mask[:, 1, :], start=False, stop=True).then_inc(rank_ps, 1)

            def gather(b):
                for k in range(KT):
                    for i in range(3):
                        for t in range(NT):
                            ins = T.matmul(bank[4][:, k * CAP:(k + 1) * CAP], xs[i][:, t, k * P:(k + 1) * P], sel[b][:, t, :],
                                           start=(i == 0 and t == 0), stop=(i == 2 and t == NT - 1))
                ins.then_inc(xg_ps, 1)

            def spread(t, b):
                for j in range(2):
                    r0 = CAP * j
                    ins = T.matmul(bank[6 + j][:], selT[b][r0:r0 + CAP, t, :], y[r0:r0 + CAP, :], start=True, stop=True)
                ins.then_inc(add_ps, 1)

            pe.wait_ge(sel_ready, 1)
            pe.wait_ge(low_ready, 2 * NT)
            pe.wait_ge(high_sb, 2 * NT)
            gather(0)
            pe.wait_ge(gatew_ready, 2)
            for t in range(NT):
                ins = T.transpose(bank[5][:, t * P:(t + 1) * P], gsel[1][:, t, :], ident)
            ins.then_inc(gT_ps, 1)
            pe.wait_ge(ld_bdown, 32)
            pe.wait_ge(bias_parts, 7)
            pe.wait_ge(bias_low, 2)
            rounds = pe.value_load(rounds_i[0:1, 0:1], min_val=1, max_val=SEQ // CAP)
            with pe.Fori(0, rounds * GROUPS) as it:
                for u in range(UNROLL):
                    n = it * UNROLL + u
                    pe.wait_ge(pick_ready, n + 1)
                    pe.wait_ge(act_sb, n + 1)
                    for f in range(2):
                        for j in range(2):
                            c0 = f * FF + j * 512
                            T.matmul(bank[f][CAP * j:CAP * (j + 1), :], pick[u % 2], bias[:, c0:c0 + 512], start=True, stop=False)
                    pe.wait_ge(xg_sb, n + 1)
                    for k in range(KT):
                        c = u * EC + k
                        pe.wait_ge(slot_full[moe_slot(c)], it * (16 * moe_turns(c)) + 16 * (moe_fills(c) + 1))
                        for f in range(2):
                            for j in range(2):
                                c0 = f * FF + j * 512
                                ins = T.matmul(bank[f][CAP * j:CAP * (j + 1), :], xg[u % 2][:, k, :], slot(moe_slot(c))[:, c0:c0 + 512],
                                               start=False, stop=(k == KT - 1))
                        ins.then_inc(chunk_used, 1)
                        if k in (2, 5):
                            t = k // 5
                            if t == 0:
                                pe.wait_ge(y_sb, n + 1)
                                pe.wait_ge(selT_sb, n + 1)
                            pe.wait_ge(add_sb, n * NT + (t + 1))
                            spread(t, (u + 1) % 2)
                        if k == 6:
                            pe.wait_ge(gsel_ready, n + 1)
                            for t in range(NT):
                                ins = T.transpose(bank[5][:, t * P:(t + 1) * P], gsel[u % 2][:, t, :], ident)
                            ins.then_inc(selT_ps, 1)
                    pe.wait_ge(sel_ready, n + 2)
                    gather((u + 1) % 2)
                    pe.wait_ge(act_sb, n + 2)
                    for jj in range(2):
                        for i in range(2):
                            b = 2 * jj + i
                            ins = T.transpose(bank[3][:, b * P:(b + 1) * P], act_o[:, 256 * jj + i:256 * jj + 256:2], ident)
                    ins.then_inc(actT_ps, 1)
                    pe.wait_ge(actT_sb, n + 1)
                    for c in range(4):
                        q = u * EC + KT + c
                        pe.wait_ge(slot_full[moe_slot(q)], it * (16 * moe_turns(q)) + 16 * (moe_fills(q) + 1))
                        for i in range(2):
                            for j in range(2):
                                lhs = actT[:, 2 * (c % 2) + i, CAP * (c // 2):CAP * (c // 2 + 1)]
                                ins = T.matmul(bank[2][CAP * j:CAP * (j + 1), :], lhs,
                                               slot(moe_slot(q))[:, i * D + j * 512:i * D + (j + 1) * 512],
                                               start=(c == 0 and i == 0), stop=(c == 3 and i == 1))
                        ins.then_inc(chunk_used, 1)
            pe.wait_ge(y_sb, rounds * E + 1)
            pe.wait_ge(add_sb, rounds * (E * NT) + 1)
            pe.wait_ge(selT_sb, rounds * E + 1)
            pe.wait_ge(act_sb, rounds * E + 1)
            for i in range(2 * NT):
                t, j = divmod(i, 2)
                r0 = CAP * j
                T.matmul(bank[(6, 0)[t] + j][:], selT[1][r0:r0 + CAP, t, :], y[r0:r0 + CAP, :],
                         start=True, stop=True).then_inc(last_ps, 1)
_INS = ["w_in", "w_out", "w_gate_up", "b_gate_up", "w_down", "b_down"]


def layout(v):
    named = {n: np.ascontiguousarray(v[n]) for n in _INS}
    seq = np.concatenate([v["meta_tokens"], v["x"][0]], 0)
    named["x"] = np.ascontiguousarray(v["x"][0])
    named["xT"] = np.ascontiguousarray(seq.T.reshape(KT, P, KEYS).transpose(1, 0, 2))
    named["x_first"] = np.ascontiguousarray(seq[:32])
    named["g_mix"] = np.ascontiguousarray(v["norm_mix_g"].reshape(KT, P).T)
    named["small_table"] = small_table(v)
    named["mixer_table"] = mixer_table()
    return named


def kernel(**inputs):
    import concourse.bacc as _bacc
    from concourse.bass_utils import run_bass_kernel_spmd as _run

    nc = _bacc.Bacc("TRN2", target_bir_lowering=False, num_devices=1)
    arrays, aps = {}, {}
    for name, arr in layout({k: np.asarray(a) for k, a in inputs.items()}).items():
        arrays[f"in_{name}"] = arr
        aps[name] = nc.dram_tensor(f"in_{name}", arr.shape, mybir.dt.from_np(arr.dtype), kind="ExternalInput").ap()
    aps["out"] = nc.dram_tensor("out_0", (1, SEQ, D), F32, kind="ExternalOutput").ap()
    build(nc, aps)
    r = _run(nc, [arrays], core_ids=[0])
    return r.results[0]["out_0"]
```
